# Optimizing a Trainium2 kernel written in Bass

```python
import jax, jax.numpy as jnp
from jax import lax
import numpy as np

D_MODEL = 1024
BATCH = 1
SEQ = 512
DEPTH = 1

D_CONV = D_MODEL
CONV_A_WIDTH = 3
EXPAND = 2
D_INNER = EXPAND * D_MODEL
HEAD_DIM = 64
N_HEADS = D_INNER // HEAD_DIM
N_GROUPS = 4
D_STATE = 128
SSD_CONV_WIDTH = 4
CHUNK = 128
D_XBC = D_INNER + 2 * N_GROUPS * D_STATE
D_FF = 2816
FFN_CONV_WIDTH = 3
N_IN = 2 * D_MODEL + 3 * D_CONV + D_INNER + D_XBC + N_HEADS
EPS = 1e-5
DT_MIN = 1e-3
DT_MAX = 1e-1


def rmsnorm(x, w):
    xf = x.astype(jnp.float32)
    y = xf * lax.rsqrt(jnp.mean(xf * xf, axis=-1, keepdims=True) + EPS)
    return (y * w.astype(jnp.float32)).astype(x.dtype)

def causal_dwconv(x, w):
    k, c = w.shape
    return lax.conv_general_dilated(
        x, w[:, None, :].astype(x.dtype), window_strides=(1,), padding=[(k - 1, 0)],
        dimension_numbers=("NWC", "WIO", "NWC"), feature_group_count=c)

def ssd_chunked_scan(xh, dt, a, bmat, cmat):
    b, s, h, p = xh.shape
    g, n = bmat.shape[-2:]
    j = h // g
    c = s // CHUNK
    x_ = (xh.astype(jnp.float32) * dt[..., None]).reshape(b, c, CHUNK, g, j, p)
    log_a = jnp.moveaxis((dt * a).reshape(b, c, CHUNK, g, j), 2, -1)
    bc = bmat.astype(jnp.float32).reshape(b, c, CHUNK, g, n)
    cc = cmat.astype(jnp.float32).reshape(b, c, CHUNK, g, n)
    a_cum = jnp.cumsum(log_a, axis=-1)

    causal = jnp.tril(jnp.ones((CHUNK, CHUNK), dtype=bool))
    seg = a_cum[..., :, None] - a_cum[..., None, :]
    decay_in = jnp.exp(jnp.where(causal, seg, -jnp.inf))
    cb = jnp.einsum("bclgn,bcsgn->bcgls", cc, bc)
    y_diag = jnp.einsum("bcgjls,bcsgjp->bclgjp", cb[:, :, :, None] * decay_in, x_)

    decay_to_end = jnp.exp(a_cum[..., -1:] - a_cum)
    states = jnp.einsum("bclgn,bcgjl,bclgjp->bcgjpn", bc, decay_to_end, x_)
    chunk_decay = jnp.exp(a_cum[..., -1])

    def step(carry, inp):
        st, dec = inp
        return carry * dec[..., None, None] + st, carry

    init = jnp.zeros((b, g, j, p, n), jnp.float32)
    _, prev = lax.scan(step, init, (jnp.moveaxis(states, 1, 0), jnp.moveaxis(chunk_decay, 1, 0)))
    prev = jnp.moveaxis(prev, 0, 1)
    y_off = jnp.einsum("bclgn,bcgjpn,bcgjl->bclgjp", cc, prev, jnp.exp(a_cum))
    return (y_diag + y_off).reshape(b, s, h, p)

def gated_group_rmsnorm(y, z, w):
    bsz, s, d = y.shape
    yf = (y.astype(jnp.float32) * jax.nn.silu(z.astype(jnp.float32))).reshape(bsz, s, N_GROUPS, d // N_GROUPS)
    yf = yf * lax.rsqrt(jnp.mean(yf * yf, axis=-1, keepdims=True) + EPS)
    return (yf.reshape(bsz, s, d) * w.astype(jnp.float32)).astype(y.dtype)

def hybrid_mixer(u, w_in, conv_a_w, w_a_out, ssd_conv_w, ssd_conv_b, dt_bias, a_log,
                 d_skip, ssd_norm_w, w_s_out, w_o):
    bsz, s, _ = u.shape
    proj = u @ w_in
    sizes = [D_MODEL, D_MODEL, D_CONV, D_CONV, D_CONV, D_INNER, D_XBC, N_HEADS]
    offsets = np.cumsum(sizes)[:-1].tolist()
    gate_a, gate_s, b_a, c_a, v_a, z, xbc, dt_raw = jnp.split(proj, offsets, axis=-1)

    y_a = (b_a * causal_dwconv(c_a * v_a, conv_a_w)) @ w_a_out

    xbc = jax.nn.silu(causal_dwconv(xbc, ssd_conv_w) + ssd_conv_b)
    xs, bs, cs = jnp.split(xbc, [D_INNER, D_INNER + N_GROUPS * D_STATE], axis=-1)
    xh = xs.reshape(bsz, s, N_HEADS, HEAD_DIM)
    dt = jax.nn.softplus(dt_raw.astype(jnp.float32) + dt_bias.astype(jnp.float32))
    a = -jnp.exp(a_log.astype(jnp.float32))
    y = ssd_chunked_scan(xh, dt, a,
                         bs.reshape(bsz, s, N_GROUPS, D_STATE),
                         cs.reshape(bsz, s, N_GROUPS, D_STATE))
    y = y + d_skip.astype(jnp.float32)[:, None] * xh.astype(jnp.float32)
    y = y.reshape(bsz, s, D_INNER).astype(u.dtype)
    y_s = gated_group_rmsnorm(y, z, ssd_norm_w) @ w_s_out

    merged = jax.nn.sigmoid(gate_a) * y_a + jax.nn.sigmoid(gate_s) * y_s
    return merged @ w_o

def conv_gated_mlp(v, w_up, ffn_conv_w, ffn_conv_b, w_down):
    hv = v @ w_up
    h1, h3 = jnp.split(hv, 2, axis=-1)
    h1 = causal_dwconv(h1, ffn_conv_w) + ffn_conv_b
    return (jax.nn.silu(h1) * h3) @ w_down

def first_inputs(seed: int = 0) -> dict:
    key = jax.random.key(seed)
    ks = jax.random.split(key, 24)
    f32 = jnp.float32

    def nrm(k, shape, scale):
        return jax.random.normal(k, shape, f32) * scale

    dt0 = jnp.exp(jax.random.uniform(ks[9], (DEPTH, N_HEADS), f32)
                  * (np.log(DT_MAX) - np.log(DT_MIN)) + np.log(DT_MIN))
    dt_bias = dt0 + jnp.log(-jnp.expm1(-dt0))
    return {
        "x": nrm(ks[0], (BATCH, SEQ, D_MODEL), 1.0),
        "norm_mix_w": 1.0 + nrm(ks[1], (DEPTH, D_MODEL), 0.02),
        "w_in": nrm(ks[2], (DEPTH, D_MODEL, N_IN), D_MODEL ** -0.5),
        "conv_a_w": nrm(ks[3], (DEPTH, CONV_A_WIDTH, D_CONV), CONV_A_WIDTH ** -0.5),
        "w_a_out": nrm(ks[4], (DEPTH, D_CONV, D_MODEL), D_CONV ** -0.5),
        "ssd_conv_w": nrm(ks[5], (DEPTH, SSD_CONV_WIDTH, D_XBC), SSD_CONV_WIDTH ** -0.5),
        "ssd_conv_b": nrm(ks[6], (DEPTH, D_XBC), 0.02),
        "dt_bias": dt_bias,
        "a_log": jnp.log(jax.random.uniform(ks[7], (DEPTH, N_HEADS), f32, 1.0, 16.0)),
        "d_skip": 1.0 + nrm(ks[8], (DEPTH, N_HEADS), 0.02),
        "ssd_norm_w": 1.0 + nrm(ks[10], (DEPTH, D_INNER), 0.02),
        "w_s_out": nrm(ks[11], (DEPTH, D_INNER, D_MODEL), D_INNER ** -0.5),
        "w_o": nrm(ks[12], (DEPTH, D_MODEL, D_MODEL), D_MODEL ** -0.5),
        "norm_ffn_w": 1.0 + nrm(ks[13], (DEPTH, D_MODEL), 0.02),
        "w_up": nrm(ks[14], (DEPTH, D_MODEL, 2 * D_FF), D_MODEL ** -0.5),
        "ffn_conv_w": nrm(ks[15], (DEPTH, FFN_CONV_WIDTH, D_FF), FFN_CONV_WIDTH ** -0.5),
        "ffn_conv_b": nrm(ks[16], (DEPTH, D_FF), 0.02),
        "w_down": nrm(ks[17], (DEPTH, D_FF, D_MODEL), D_FF ** -0.5),
        "final_norm_w": 1.0 + nrm(ks[18], (D_MODEL,), 0.02),
    }

def first_block(x, norm_mix_w, w_in, conv_a_w, w_a_out, ssd_conv_w, ssd_conv_b, dt_bias,
              a_log, d_skip, ssd_norm_w, w_s_out, w_o, norm_ffn_w, w_up, ffn_conv_w,
              ffn_conv_b, w_down, final_norm_w):
    h = x
    for l in range(DEPTH):
        u = rmsnorm(h, norm_mix_w[l])
        h = h + hybrid_mixer(u, w_in[l], conv_a_w[l], w_a_out[l], ssd_conv_w[l], ssd_conv_b[l],
                             dt_bias[l], a_log[l], d_skip[l], ssd_norm_w[l], w_s_out[l], w_o[l])
        v = rmsnorm(h, norm_ffn_w[l])
        h = h + conv_gated_mlp(v, w_up[l], ffn_conv_w[l], ffn_conv_b[l], w_down[l])
    return rmsnorm(h, final_norm_w)


HGRN_KDIM = 128
HGRN_VDIM = 128
HGRN_HEADS = D_MODEL // HGRN_KDIM
HGRN_WIDTH = HGRN_HEADS * HGRN_KDIM
GLA_CHUNK = 64
SG_CHUNK = 128
SG_GROUP_CH = 128
SG_GROUPS = D_MODEL // SG_GROUP_CH
SG_WIDTH = SG_GROUPS * SG_GROUP_CH
IN_SPLITS = (HGRN_WIDTH, HGRN_WIDTH, HGRN_WIDTH, HGRN_WIDTH, HGRN_WIDTH,
             SG_WIDTH, SG_WIDTH, SG_WIDTH, D_MODEL, D_MODEL)
IN_WIDTH = 5 * HGRN_WIDTH + 3 * SG_WIDTH + 2 * D_MODEL
RMS_EPS = 1e-6
LN_EPS = 1e-5
LB_FLOOR = 1e-20


def _rmsnorm(x, w, eps=RMS_EPS):
    xf = x.astype(jnp.float32)
    y = xf * lax.rsqrt(jnp.mean(xf * xf, axis=-1, keepdims=True) + eps)
    return (y * w.astype(jnp.float32)).astype(x.dtype)

def _layernorm(x, w, b, eps=LN_EPS):
    xf = x.astype(jnp.float32)
    mu = jnp.mean(xf, axis=-1, keepdims=True)
    var = jnp.mean(jnp.square(xf - mu), axis=-1, keepdims=True)
    y = (xf - mu) * lax.rsqrt(var + eps)
    return (y * w.astype(jnp.float32) + b.astype(jnp.float32)).astype(x.dtype)

def _gla_chunked(q, k, v, log_f):
    b, h, s, dk = q.shape
    dv = v.shape[-1]
    n = s // GLA_CHUNK

    def to_chunks(t):
        return jnp.moveaxis(t.reshape(b, h, n, GLA_CHUNK, t.shape[-1]), 2, 0)

    qc, kc, vc = to_chunks(q), to_chunks(k), to_chunks(v)
    gc = jnp.cumsum(to_chunks(log_f), axis=-2)
    mask = jnp.tril(jnp.ones((GLA_CHUNK, GLA_CHUNK), dtype=bool))[:, :, None]

    def step(state, xs):
        qb, kb, vb, gb = xs
        diff = gb[..., :, None, :] - gb[..., None, :, :]
        decay = jnp.where(mask, jnp.exp(jnp.where(mask, diff, 0.0)), 0.0)
        attn = jnp.einsum('bhtd,bhsd,bhtsd->bhts', qb, kb, decay)
        o = jnp.einsum('bhts,bhsv->bhtv', attn, vb)
        o = o + jnp.einsum('bhtd,bhdv->bhtv', qb * jnp.exp(gb), state)
        g_last = gb[..., -1:, :]
        k_dec = kb * jnp.exp(g_last - gb)
        state = state * jnp.exp(g_last[..., 0, :])[..., None] + jnp.einsum('bhsd,bhsv->bhdv', k_dec, vb)
        return state, o

    state0 = jnp.zeros((b, h, dk, dv), jnp.float32)
    _, outs = lax.scan(step, state0, (qc, kc, vc, gc))
    return jnp.moveaxis(outs, 0, 2).reshape(b, h, s, dv)

def _hgrn2_forget(f_raw, lb):
    z = f_raw.astype(jnp.float32)
    k = (1.0 - lb) * jax.nn.sigmoid(-z)
    log_f = jnp.logaddexp(jnp.log(jnp.maximum(lb, LB_FLOOR)),
                          jnp.log1p(-lb) + jax.nn.log_sigmoid(z))
    return k, log_f

def _hgrn2_branch(q_raw, ffwd_raw, fbwd_raw, i_raw, g_raw, lb_fwd, lb_bwd, gnorm_w):
    b, s, _ = q_raw.shape

    def heads(t):
        return t.reshape(b, s, HGRN_HEADS, -1).transpose(0, 2, 1, 3).astype(jnp.float32)

    def flip(t):
        return jnp.flip(t, axis=2)

    q = heads(jax.nn.silu(q_raw)) * (HGRN_KDIM ** -0.5)
    v = heads(i_raw)
    k_f, g_f = _hgrn2_forget(ffwd_raw, lb_fwd)
    k_b, g_b = _hgrn2_forget(fbwd_raw, lb_bwd)
    o_fwd = _gla_chunked(q, heads(k_f), v, heads(g_f))
    o_bwd = flip(_gla_chunked(flip(q), flip(heads(k_b)), flip(v), flip(heads(g_b))))
    o = (o_fwd + o_bwd).transpose(0, 2, 1, 3)
    o = _rmsnorm(o, gnorm_w).reshape(b, s, HGRN_HEADS * HGRN_VDIM)
    return (o * jax.nn.silu(g_raw.astype(jnp.float32))).astype(q_raw.dtype)

def _spatial_gating_branch(u_raw, v_raw, g_raw, ln_w, ln_b, w_s, b_s):
    b, s, _ = u_raw.shape
    u = jax.nn.gelu(u_raw)
    v = _layernorm(jax.nn.gelu(v_raw), ln_w, ln_b)
    vc = v.reshape(b, s // SG_CHUNK, SG_CHUNK, SG_GROUPS, SG_GROUP_CH)
    mixed = jnp.einsum('gts,bnsgc->bntgc', w_s, vc) + b_s.T[None, None, :, :, None]
    return u * mixed.reshape(b, s, SG_WIDTH) * jax.nn.silu(g_raw)

def second_inputs(seed: int = 0) -> dict:
    key = jax.random.key(seed)
    ks = jax.random.split(key, 16)
    f32 = jnp.float32
    x = jax.random.normal(ks[0], (BATCH, SEQ, D_MODEL), f32)
    norm_w = 1.0 + 0.05 * jax.random.normal(ks[1], (DEPTH, D_MODEL), f32)
    w_in = jax.random.normal(ks[2], (DEPTH, D_MODEL, IN_WIDTH), f32) * D_MODEL ** -0.5
    lower_bounds = 0.1 * jax.random.normal(ks[3], (DEPTH, 2, HGRN_WIDTH), f32)
    gnorm_w = 1.0 + 0.05 * jax.random.normal(ks[4], (DEPTH, HGRN_VDIM), f32)
    ln_w = 1.0 + 0.05 * jax.random.normal(ks[5], (DEPTH, SG_WIDTH), f32)
    ln_b = 0.02 * jax.random.normal(ks[6], (DEPTH, SG_WIDTH), f32)
    w_s = jax.random.normal(ks[7], (DEPTH, SG_GROUPS, SG_CHUNK, SG_CHUNK), f32) * SG_CHUNK ** -0.5
    b_s = 1.0 + 0.1 * jax.random.normal(ks[8], (DEPTH, SG_GROUPS, SG_CHUNK), f32)
    w_proj_a = jax.random.normal(ks[9], (DEPTH, HGRN_WIDTH, D_MODEL), f32) * HGRN_WIDTH ** -0.5
    w_proj_b = jax.random.normal(ks[10], (DEPTH, SG_WIDTH, D_MODEL), f32) * SG_WIDTH ** -0.5
    w_out = jax.random.normal(ks[11], (DEPTH, D_MODEL, D_MODEL), f32) * D_MODEL ** -0.5
    final_norm_w = 1.0 + 0.05 * jax.random.normal(ks[12], (D_MODEL,), f32)
    return {"x": x, "norm_w": norm_w, "w_in": w_in, "lower_bounds": lower_bounds,
            "gnorm_w": gnorm_w, "ln_w": ln_w, "ln_b": ln_b, "w_s": w_s, "b_s": b_s,
            "w_proj_a": w_proj_a, "w_proj_b": w_proj_b, "w_out": w_out,
            "final_norm_w": final_norm_w}

def second_block(x, norm_w, w_in, lower_bounds, gnorm_w, ln_w, ln_b, w_s, b_s,
              w_proj_a, w_proj_b, w_out, final_norm_w):
    lb = jax.nn.softmax(lower_bounds.astype(jnp.float32), axis=0)
    lb = jnp.cumsum(lb, axis=0) - lb[0]
    split_points = []
    acc = 0
    for size in IN_SPLITS[:-1]:
        acc += size
        split_points.append(acc)
    for layer in range(DEPTH):
        h = _rmsnorm(x, norm_w[layer])
        proj = jnp.einsum('bsd,de->bse', h, w_in[layer])
        (q_raw, ffwd_raw, fbwd_raw, i_raw, ga_raw,
         u_raw, v_raw, gb_raw, ma_raw, mb_raw) = jnp.split(proj, split_points, axis=-1)
        y_a = _hgrn2_branch(q_raw, ffwd_raw, fbwd_raw, i_raw, ga_raw,
                            lb[layer, 0], lb[layer, 1], gnorm_w[layer])
        y_b = _spatial_gating_branch(u_raw, v_raw, gb_raw, ln_w[layer], ln_b[layer],
                                     w_s[layer], b_s[layer])
        merged = (jax.nn.sigmoid(ma_raw) * jnp.einsum('bsw,wd->bsd', y_a, w_proj_a[layer])
                  + jax.nn.sigmoid(mb_raw) * jnp.einsum('bsw,wd->bsd', y_b, w_proj_b[layer]))
        x = x + jnp.einsum('bsd,de->bse', merged, w_out[layer])
    return _rmsnorm(x, final_norm_w)


def setup_inputs(seed=0):
    out = dict(first_inputs(seed))
    for name, value in second_inputs(seed + 1).items():
        if name != "x":
            out[name + "_2"] = value
    return out


def reference(
    x, norm_mix_w, w_in, conv_a_w, w_a_out, ssd_conv_w, ssd_conv_b, dt_bias, a_log, d_skip,
    ssd_norm_w, w_s_out, w_o, norm_ffn_w, w_up, ffn_conv_w, ffn_conv_b, w_down, final_norm_w,
    norm_w_2, w_in_2, lower_bounds_2, gnorm_w_2, ln_w_2, ln_b_2, w_s_2, b_s_2, w_proj_a_2,
    w_proj_b_2, w_out_2, final_norm_w_2,
):
    x = first_block(
        x, norm_mix_w, w_in, conv_a_w, w_a_out, ssd_conv_w, ssd_conv_b, dt_bias, a_log, d_skip,
        ssd_norm_w, w_s_out, w_o, norm_ffn_w, w_up, ffn_conv_w, ffn_conv_b, w_down,
        final_norm_w,
    )
    return second_block(
        x, norm_w_2, w_in_2, lower_bounds_2, gnorm_w_2, ln_w_2, ln_b_2, w_s_2, b_s_2,
        w_proj_a_2, w_proj_b_2, w_out_2, final_norm_w_2,
    )


_drawn_inputs = setup_inputs


def setup_inputs(seed=0):
    import zlib

    import numpy as np

    out = dict(_drawn_inputs(seed))
    spreads = {}
    factors = {'ssd_conv_b': 3.712,
     'd_skip': 7.921,
     'ssd_norm_w': 5.303,
     'norm_ffn_w': 3.828,
     'ffn_conv_b': 5.904,
     'gnorm_w_2': 4.373,
     'ln_w_2': 6.084,
     'ln_b_2': 30.778,
     'b_s_2': 2.825}
    for name, (base, spread) in spreads.items():
        noise = np.random.default_rng([zlib.crc32(name.encode()), seed]).standard_normal(out[name].shape)
        drawn = base * np.exp(spread * noise) if base else spread * noise
        out[name] = __import__('jax').numpy.asarray(drawn.astype(out[name].dtype))
    for name, factor in factors.items():
        out[name] = (out[name] * factor).astype(out[name].dtype)
    return out
```

```python
from contextlib import ExitStack

import numpy as np

import concourse.bass as bass
from concourse import mybir

P = 128
T = 512
D = 1024
KT = D // P
D_INNER = 2 * D
HEADS = 32
HEAD_DIM = 64
GROUPS = 4
D_STATE = 128
D_XBC = D_INNER + 2 * GROUPS * D_STATE
D_FF = 2816
FT = D_FF // P
NCH = T // P
EPS = 1e-5
RMS_EPS = 1e-6
LN_EPS = 1e-5
LB_FLOOR = 1e-20
RING = 4
AHEAD = 2
LEVELS = (64, 32, 16, 8, 4)
BOTTOM = 4

F32 = mybir.dt.float32
F32R = mybir.dt.float32r
U8 = mybir.dt.uint8
ALU = mybir.AluOpType
ACT = mybir.ActivationFunctionType

GATE_A, GATE_S, B_A, C_A, V_A, Z, XBC = np.cumsum([0, D, D, D, D, D, D_INNER]).tolist()
DT = XBC + D_XBC
Q2, FF2, FB2, I2, GA2, U2, V2, GB2, MA2, MB2 = (D * k for k in range(10))

PARAMS = [
    ("norm_mix_w", KT), ("conv_a_w", 3 * KT), ("ssd_conv_w", 4 * D_XBC // P), ("ssd_conv_b", D_XBC // P),
    ("dt_bias", 1), ("a_log", 1), ("d_skip", D_INNER // P), ("ssd_norm_w", D_INNER // P),
    ("norm_ffn_w", KT), ("ffn_conv_w", 3 * FT), ("ffn_conv_b", FT), ("final_norm_w", KT),
    ("norm_w_2", KT), ("lower_bounds_2", 2 * KT), ("gnorm_w_2", 1), ("ln_w_2", KT), ("ln_b_2", KT),
    ("final_norm_w_2", KT),
]
PCOL = dict(zip([n for n, _ in PARAMS], np.cumsum([0] + [c for _, c in PARAMS]).tolist()))
NPAR = sum(c for _, c in PARAMS)

PHASES = [
    ("conv_a", 2, 12, 12, 0), ("dt", 1, 1, 1, 0), ("gate_a", 2, 4, 4, 0), ("w_a_out", 2, 4, 0, 4),
    ("ssd", 2, 20, 20, 0), ("gate_s", 2, 4, 4, 0), ("w_s_out", 4, 4, 0, 2), ("w_o", 2, 4, 0, 4),
    ("w_up", 11, 4, 4, 0), ("w_down", 2, 12, 0, 4),
    ("sg_v", 2, 4, 4, 0), ("sg_u", 2, 4, 4, 0), ("sg_gb", 2, 4, 4, 0), ("mb", 2, 4, 4, 0), ("proj_b", 2, 4, 0, 4),
    ("gla", 4, 12, 12, 0), ("proj_a", 2, 4, 0, 4), ("w_out", 2, 4, 0, 4),
]


class Span:

    def __init__(self, n0, a0, d0, phase):
        self.n0, self.a0, self.d0 = n0, a0, d0
        self.name, self.iters, self.blocks, self.atiles, self.dtiles = phase


def spans():
    out, n, a, d = {}, 0, 0, 0
    for ph in PHASES:
        out[ph[0]] = Span(n, a, d, ph)
        n, a, d = n + ph[1] * ph[2], a + ph[1] * ph[3], d + ph[1] * ph[4]
    return out, n


ROLLED = [name for name, iters, *_ in PHASES if iters > 1 and name != PHASES[-1][0]]
SPANS, NBLK = spans()


def build(nc, x_in, wall, par_in, consts_in, masks_in, ws_in, bs_in, out):
    ctx = ExitStack()
    with ctx:
        base = [-(-nc.sbuf_base // 64) * 64]

        def place(name, shape, dtype, at):
            return nc.alloc_sbuf_tensor_at(name, shape, dtype, offset=at)

        def fixed(name, shape, dtype):
            size = int(np.prod(shape[1:])) * (1 if dtype == U8 else 4)
            at = base[0]
            base[0] += -(-size // 64) * 64
            return place(name, shape, dtype, at)

        def sem(name):
            return ctx.enter_context(nc.semaphore(name))

        raw = fixed("raw", [P, RING, KT, P], F32)
        w_high = fixed("w_high", [P, RING, KT, P], F32R)
        w_low = fixed("w_low", [P, RING, KT, P], F32R)
        X = fixed("X", [P, KT, T], F32)
        act_at = base[0]
        u_high = fixed("u_high", [P, KT, T], F32R)
        u_low = fixed("u_low", [P, KT, T], F32R)
        par = fixed("par", [P, NPAR], F32)
        cst = fixed("cst", [P, 3, P], F32)
        ident, ones, upper = cst[:, 0], cst[:, 1], cst[:, 2]
        identR = fixed("identR", [P, P], F32R)
        masks = fixed("masks", [P, 2, len(LEVELS) * T // 2 + T], U8)
        tok = fixed("tok", [P, 3, NCH, HEADS], F32)
        decay_b = fixed("decay_b", [P, NCH, HEADS], F32)
        acum_high = fixed("acum_high", [HEADS, T], F32R)
        acum_low = fixed("acum_low", [HEADS, T], F32R)
        ws_t = place("ws_t", [P, KT, P], F32, base[0] - 2 * 4 * T)
        pick = fixed("pick", [HEADS, 2, HEADS // GROUPS], F32R)
        lbc = fixed("lbc", [P, 6, 2 * KT], F32)
        eps = fixed("eps", [P, 4], F32)
        sums = fixed("sums", [P, T], F32)
        F = base[0]
        free = nc.sbuf_usable_end - F
        K = 1024

        def pcol(name, k=0):
            return par[:, PCOL[name] + k:PCOL[name] + k + 1]


        M = place("M", [P, KT, T], F32, F)
        masks_f = place("masks_f", [P, 2, len(LEVELS) * T // 2 + T], F32, F)
        a_high = place("a_high", [P, KT, T], F32R, F + 16 * K)
        a_low = place("a_low", [P, KT, T], F32R, F + 32 * K)
        Y = place("Y", [P, 2 * KT, T], F32, F + 16 * K)
        m_high = place("m_high", [P, KT, T], F32R, F + 16 * K)
        m_low = place("m_low", [P, KT, T], F32R, F + 32 * K)
        t0 = F + 48 * K
        stage = place("stage", [P, 2, 3, T], F32, t0)
        conv_p = place("conv_p", [P, T], F32, t0 + 12 * K)
        conv_o = place("conv_o", [P, T], F32, t0 + 14 * K)
        norm_t = place("norm_t", [P, T], F32, t0 + 16 * K)
        root = place("root", [P, T], F32, t0 + 18 * K)
        rstd = place("rstd", [P, T], F32, t0 + 20 * K)
        dtw = place("dtw", [HEADS, 8, T], F32, t0 + 22 * K)
        dsmall = place("dsmall", [HEADS, 2, NCH * HEADS], F32, t0 + 38 * K)
        raw_x = place("raw_x", [P, 2, T], F32, t0)
        Bc = place("Bc", [P, T], F32, t0 + 4 * K)
        Cc = place("Cc", [P, T], F32, t0 + 6 * K)
        Btok = place("Btok", [P, NCH, P], F32, t0 + 8 * K)
        CBm = place("CBm", [P, NCH, P], F32, t0 + 10 * K)
        xs = place("xs", [P, 2, T], F32, t0 + 12 * K)
        xdt = place("xdt", [P, NCH, T], F32, t0 + 16 * K)
        xdec = place("xdec", [P, NCH - 1, T], F32, t0 + 24 * K)
        seg = place("seg", [P, 2, T], F32, t0 + 30 * K)
        cexp = place("cexp", [P, 2, T], F32, t0 + 34 * K)
        gsum = place("gsum", [P, GROUPS, T], F32, t0 + 38 * K)
        sig_s = place("sig_s", [P, KT, T], F32, t0)
        groot = place("groot", [P, GROUPS, T], F32, t0 + 16 * K)
        y_high = place("y_high", [P, 2 * KT, T], F32R, t0 + 16 * K)
        y_low = place("y_low", [P, 2 * KT, T], F32R, act_at)

        f_high = place("f_high", [P, FT, T], F32R, F)
        f_low = place("f_low", [P, FT, T], F32R, F + 44 * K)
        h1_raw = place("h1_raw", [P, T], F32, F + 88 * K)
        h1_conv = place("h1_conv", [P, T], F32, F + 90 * K)
        h3_raw = place("h3_raw", [P, T], F32, F + 92 * K)
        root_late = place("root_late", [P, T], F32, F + 90 * K)
        norm_f = place("norm_f", [P, T], F32, F + 88 * K)
        VG = place("VG", [P, KT, T], F32, F)
        UG = place("UG", [P, KT, T], F32, F + 16 * K)
        b_high = place("b_high", [P, KT, T], F32R, F + 32 * K)
        b_low = place("b_low", [P, KT, T], F32R, F + 48 * K)
        M2 = place("M2", [P, KT, T], F32, F + 64 * K)
        vn = place("vn", [P, 2, T], F32, F + 80 * K)
        vt = place("vt", [P, 2, NCH, P], F32, F + 84 * K)
        ln_a = place("ln_a", [P, T], F32, F + 88 * K)
        ln_b = place("ln_b", [P, T], F32, F + 90 * K)
        bs_row = place("bs_row", [1, KT, P], F32, F + 92 * K)
        Ya = place("Ya", [P, KT, T], F32, F)
        SA = place("SA", [P, KT, T], F32, F + 16 * K)
        R = place("R", [P, 5, T], F32, F + 32 * K)
        Kd = place("Kd", [P, 2, T], F32, F + 42 * K)
        G = place("G", [P, 2, T], F32, F + 46 * K)
        v_tok = place("v_tok", [P, NCH, P], F32, F + 50 * K)
        att = place("att", [P, 2, T], F32, F + 52 * K)
        XL = place("XL", [P, 4, T], F32, F + 56 * K)
        Sd = place("Sd", [P, 2, NCH - 1, P], F32, F + 80 * K)
        k_tok = place("k_tok", [P, NCH - 1, P], F32, F + 83 * K)
        tot = place("tot", [P, 2, NCH], F32, F + 84 * K + 512)
        dtot = place("dtot", [P, 2, NCH], F32, F + 84 * K + 544)
        rsum = place("rsum", [P, T // BOTTOM], F32, F + 84 * K + 1024)
        resets = place("resets", [P, T], F32, F + 86 * K)
        head_o = place("head_o", [P, T], F32, F + 88 * K)
        head_s = place("head_s", [P, T], F32, F + 90 * K)
        ya_high = place("ya_high", [P, KT, T], F32R, F + 32 * K)
        ya_low = place("ya_low", [P, KT, T], F32R, F + 48 * K)
        n_high = place("n_high", [P, KT, T], F32R, F)
        norm_e = place("norm_e", [P, T], F32, F + 88 * K)
        assert F + 96 * K <= nc.sbuf_usable_end, (F, nc.sbuf_usable_end)

        ps = [ctx.enter_context(nc.psum_tensor(f"bank{k}", [P, T], F32)) for k in range(8)]
        accA, accD, side = ps[0:2], ps[2:4], ps[4:8]

        landed = [sem(f"landed{s}") for s in range(RING)]
        hi_done, lo_done, block_done = sem("hi_done"), sem("lo_done"), sem("block_done")
        evacA, evacD = sem("evacA"), sem("evacD")
        s_par, s_x, s_cst, s_out = sem("s_par"), sem("s_x"), sem("s_cst"), sem("s_out")
        vstep, astep = sem("vstep"), sem("astep")
        s_init, s_fin = sem("s_init"), sem("s_fin")
        s_sq, s_stat, s_root, s_split = sem("s_sq"), sem("s_stat"), sem("s_root"), sem("s_split")
        a_used, a_split = sem("a_used"), sem("a_split")
        d_raw, d_ln, d_acum, d_exp, d_done, d_turned, d_tok = (
            sem(f"dt_{k}") for k in "raw ln acum exp done turned tok".split())
        c_ready, c_used, c_silu = sem("conv_ready"), sem("conv_used"), sem("conv_silu")
        s_turned, s_cb, s_taken = sem("ssd_turned"), sem("ssd_cb"), sem("ssd_taken")
        s_scaled, s_carry, s_pick = sem("ssd_scaled"), sem("ssd_carry"), sem("ssd_pick")
        s_seg, s_min, s_exp, s_mat, s_y, s_ytaken = (sem(f"ssd_{k}") for k in "seg min exp mat y ytaken".split())
        g_sq, g_stat, g_root, y_split, m_split = (sem(k) for k in "g_sq g_stat g_root y_split m_split".split())

        f_conv, f_silu, f_used, f_split = (sem(f"mlp_{k}") for k in "conv silu used split".split())
        s_ws = sem("s_ws")
        v_sum, v_mean, v_mu, v_sq, v_var, v_root = (sem(f"ln_{k}") for k in "sum mean mu sq var root".split())
        gs_used, vn_done, vn_turned, vt_done, s_mix, b_split = (
            sem(f"sg_{k}") for k in "gsused vn turned vt mix split".split())
        x_clear = sem("hg_clear")
        lb_a, lb_v = sem("lb_a"), sem("lb_v")
        r_used, l_ln, l_k, l_floor, v_turned, v_taken = (
            sem(f"hg_{k}") for k in "used ln k floor vturned vtaken".split())
        x_diff, x_exp, x_pair, x_mm, x_put = (sem(f"hg_{k}") for k in "diff exp pair mm put".split())
        e_diff, e_exp, e_mul, k_turned, k_taken, st_mm, st_done = (
            sem(f"hg_{k}") for k in "ediff eexp emul kturned ktaken stmm stdone".split())
        o_mm, o_sq, o_stat, o_rstd, ya_split, n_split = (
            sem(k) for k in "o_mm o_sq o_stat o_rstd ya_split n_split".split())

        block = ctx.enter_context(nc.Block())

        class Chain:

            def __init__(self, eng, s):
                self.eng, self.s, self.base, self.per, self.i, self.k = eng, s, 0, 0, 0, 0

            def __call__(self, ins):
                self.k += 1
                ins.then_inc(self.s, 1)
                self.eng.wait_ge(self.s, self.i * self.per + (self.base + self.k))

        def loop(eng, span, body, chain=None, per=0):
            rolled = span.name in ROLLED
            if chain:
                chain.base, chain.k, chain.per = chain.base + chain.k, 0, per
            if rolled:
                with eng.Fori(0, span.iters) as i:
                    if chain:
                        chain.i = i
                    body(i)
                if chain:
                    assert chain.k == per, (span.name, chain.k, per)
                    chain.base, chain.k = chain.base + span.iters * per, 0
            else:
                for i in range(span.iters):
                    body(i)
            if chain:
                chain.per = chain.i = 0

        def blk(span, i, c):
            return i * span.blocks + (span.n0 + c)

        def tile_at(t, k, n=1):
            return t[:, bass.ds(k, n)] if not isinstance(k, int) else t[:, k:k + n]

        def one(t, k):
            if isinstance(k, int):
                return t[:, k]
            return t[:, bass.ds(k, 1)].rearrange("p o t -> p (o t)")

        def col(name, k):
            if isinstance(k, int):
                return pcol(name, k)
            return par[:, bass.ds(k + PCOL[name], 1)]

        @block.sync
        def _(sp):
            sp.dma_start(par[:], par_in).then_inc(s_par, 16)
            sp.dma_start(X[:], x_in.rearrange("(k p) t -> p k t", p=P)).then_inc(s_x, 16)
            sp.dma_start(cst[:], consts_in).then_inc(s_cst, 16)
            sp.dma_start(masks_f[:], masks_in).then_inc(s_cst, 16)
            for n in range(RING):
                sp.dma_start(raw[:, n], wall[n].rearrange("p (k c) -> p k c", k=KT)).then_inc(landed[n], 16)

            def load(n, s):
                sp.wait_ge(lo_done, n + (1 - RING))
                src = wall[n] if isinstance(n, int) else wall[bass.ds(n, 1)].rearrange("o p k -> (o p) k")
                sp.dma_start(raw[:, s], src.rearrange("p (k c) -> p k c", k=KT)).then_inc(landed[s], 16)

            with sp.Fori(1, NBLK // RING) as i:
                for s in range(RING):
                    load(i * RING + s, s)
            for n in range(NBLK // RING * RING, NBLK):
                load(n, n % RING)


        @block.tensor
        def _(pe):
            pe.sem_inc(block_done, RING)
            pe.sem_inc(s_y, 2)

            def wblock(span, i, c, moving, acc, kts=range(KT), at=0, start=True, stop=True):
                xh, xl = moving
                slot = (span.n0 + c) % RING
                pe.wait_ge(lo_done, blk(span, i, c) + 1)
                kts = list(kts)
                for k in kts:
                    for j, (w, x) in enumerate(((w_high, xh), (w_high, xl), (w_low, xh))):
                        ins = pe.matmul(acc[:], w[:, slot, k], x[:, at + k],
                                        start=start and k == kts[0] and j == 0,
                                        stop=stop and k == kts[-1] and j == 2)
                ins.then_inc(block_done, 1)

            def freeA(span, i, t):
                pe.wait_ge(evacA, i * span.atiles + (span.a0 + t + 1))

            def freeD(span, i, t):
                pe.wait_ge(evacD, i * span.dtiles + (span.d0 + t + 1))

            def stat(n):
                pe.wait_ge(s_sq, n + 1)
                pe.matmul(side[0][:], ones, sums[:], start=True, stop=True).then_inc(s_stat, 1)

            def plainA(name, moving):
                span = SPANS[name]

                def body(i):
                    for c in range(span.blocks):
                        freeA(span, i, c)
                        wblock(span, i, c, moving, accA[(span.a0 + c) % 2])
                loop(pe, span, body)

            def plainD(name, moving):
                span = SPANS[name]

                def body(i):
                    for c in range(span.blocks):
                        freeD(span, i, c)
                        wblock(span, i, c, moving, accD[(span.d0 + c) % 2])
                loop(pe, span, body)

            U = (u_high, u_low)
            pe.wait_ge(s_cst, 32)
            stat(0)
            pe.wait_ge(s_split, KT)
            plainA("conv_a", U)
            plainA("dt", U)
            plainA("gate_a", U)
            pe.wait_ge(d_done, 1)
            for j in range(3):
                for c in range(NCH):
                    k = j * NCH + c
                    pe.transpose(side[0][:, k * HEADS:(k + 1) * HEADS], dtw[:, j, c * P:(c + 1) * P],
                                 cst[0:HEADS, 0, 0:HEADS])
            pe.matmul(side[1][:, 0:NCH * HEADS], cst[0:HEADS, 1], dsmall[:, 1],
                      start=True, stop=True).then_inc(d_turned, 1)
            pe.wait_ge(a_split, KT)
            plainD("w_a_out", (a_high, a_low))

            span = SPANS["ssd"]

            def ssd_group(i, gg):
                r8, r4, r1 = i * 16 + 8 * gg, i * 8 + 4 * gg, i * 2 + gg
                turned = [0]

                def mm(c):
                    freeA(span, i, 10 * gg + c)
                    wblock(span, i, 10 * gg + c, U, accA[(span.a0 + 10 * gg + c) % 2])

                def turn(src, silu):
                    pe.wait_ge(c_silu, i * 12 + (6 * gg + silu + 1))
                    pe.wait_ge(s_taken, r8 + (turned[0] + 1))
                    for c in range(NCH):
                        ins = pe.transpose(side[3][:, c * P:(c + 1) * P], src[:, c * P:(c + 1) * P], ident)
                    ins.then_inc(s_turned, 1)
                    turned[0] += 1

                def seg_rows(h):
                    pe.wait_ge(s_exp, i * 32 + (16 * gg + 2 * h + 2))
                    for n, part in enumerate((acum_high, acum_low)):
                        ins = pe.matmul(side[h % 2][:], pick[:, gg, h:h + 1].to_broadcast([HEADS, P]), part[:],
                                        start=n == 0, stop=n == 1)
                    ins.then_inc(s_seg, 1)

                def head_y(h):
                    rows = slice(HEAD_DIM * (h % 2), HEAD_DIM * (h % 2) + HEAD_DIM)
                    hs = slice(h * HEAD_DIM, (h + 1) * HEAD_DIM)
                    if h % 2 == 0:
                        pe.wait_ge(s_ytaken, r4 + (h // 2 + 1))
                    pe.wait_ge(s_mat, i * 32 + (16 * gg + 2 * h + 2))
                    for c in range(NCH):
                        cs = slice(c * P, (c + 1) * P)
                        ins = pe.matmul(side[2][rows, cs], xdt[:, c, hs], seg[:, h % 2, cs], start=True, stop=c == 0)
                        if c:
                            ins = pe.matmul(side[2][rows, cs], xdec[:, c - 1, hs], cexp[:, h % 2, cs],
                                            start=False, stop=True)
                    ins.then_inc(s_y, 1)

                for c in range(3):
                    mm(c)
                turn(Bc, 0)
                pe.wait_ge(c_silu, i * 12 + (6 * gg + 2))
                pe.wait_ge(s_ytaken, r4 + 1)
                for c in range(NCH):
                    cs = slice(c * P, (c + 1) * P)
                    ins = pe.matmul(side[2][:, cs], Bc[:, cs], Cc[:, cs], start=True, stop=True)
                ins.then_inc(s_cb, 1)
                for j in range(4):
                    mm(3 + j)
                    turn(xs[:, j % 2], 2 + j)
                pe.wait_ge(s_pick, r1 + 1)
                seg_rows(0)
                seg_rows(1)
                for c in range(NCH - 1):
                    pe.wait_ge(s_scaled, r4 + 4)
                    pe.wait_ge(s_taken, r8 + (turned[0] + 1))
                    pe.matmul(side[3][:], Btok[:, c], xdec[:, c], start=True, stop=True).then_inc(s_turned, 1)
                    turned[0] += 1
                for j in range(3):
                    mm(7 + j)
                    for h in (2 * j, 2 * j + 1):
                        head_y(h)
                    for h in (2 * j + 2, 2 * j + 3):
                        seg_rows(h)
                for h in (6, 7):
                    head_y(h)

            def body(i):
                for gg in range(2):
                    ssd_group(i, gg)
            loop(pe, span, body)

            for g in range(GROUPS):
                pe.wait_ge(g_sq, g + 1)
                if g == 0:
                    pe.wait_ge(g_sq, GROUPS)
                pe.matmul(side[g][:], ones, gsum[:, g], start=True, stop=True).then_inc(g_stat, 1)
            plainA("gate_s", U)
            pe.wait_ge(y_split, KT)
            span = SPANS["w_s_out"]

            def body(i):
                for t in range(2):
                    freeD(span, i, t)
                    for half in range(2):
                        pe.wait_ge(y_split, (half + 1) * KT)
                        wblock(span, i, 2 * t + half, (y_high, y_low), accD[(span.d0 + t) % 2],
                               at=half * KT, start=half == 0, stop=half == 1)
            loop(pe, span, body)
            pe.wait_ge(m_split, KT)
            plainD("w_o", (m_high, m_low))

            stat(1)
            pe.wait_ge(s_split, 2 * KT)
            plainA("w_up", U)
            pe.wait_ge(f_split, FT)
            span = SPANS["w_down"]

            def body(i):
                for t in range(4):
                    freeD(span, i, t)
                    for part in range(3):
                        wblock(span, i, 3 * t + part, (f_high, f_low), accD[(span.d0 + t) % 2],
                               kts=range(KT) if part < 2 else range(3 * KT - FT, KT),
                               at=part * KT if part < 2 else FT - KT, start=part == 0, stop=part == 2)
            loop(pe, span, body)
            stat(2)
            stat(3)
            pe.wait_ge(s_split, 3 * KT)
            plainA("sg_v", U)
            pe.wait_ge(v_sum, 1)
            pe.matmul(side[0][:], ones, sums[:], start=True, stop=True).then_inc(v_mean, 1)
            plainA("sg_u", U)
            pe.wait_ge(v_sq, 1)
            pe.matmul(side[0][:], ones, sums[:], start=True, stop=True).then_inc(v_var, 1)
            plainA("sg_gb", U)

            span = SPANS["mb"]
            pe.wait_ge(s_ws, 32)

            def body(i):
                def mix(c):
                    j = i * 4 + c
                    pe.wait_ge(vt_done, j + 1)
                    pe.wait_ge(b_split, j + 1)
                    w = ws_t[:, j] if isinstance(j, int) else ws_t[:, bass.ds(j, 1)].rearrange("p o t -> p (o t)")
                    b = bs_row[:, j] if isinstance(j, int) else bs_row[:, bass.ds(j, 1)].rearrange("p o t -> p (o t)")
                    for n in range(NCH):
                        o = side[2][:, n * P:(n + 1) * P]
                        pe.matmul(o, vt[:, c % 2, n], w, start=True, stop=False)
                        ins = pe.matmul(o, cst[0:1, 1], b, start=False, stop=True)
                    ins.then_inc(s_mix, 1)

                for c in range(span.blocks):
                    freeA(span, i, c)
                    wblock(span, i, c, U, accA[(span.a0 + c) % 2])
                    if c:
                        mix(c - 1)
                    pe.wait_ge(vn_done, i * 4 + (c + 1))
                    if c:
                        pe.wait_ge(vt_done, i * 4 + c)
                    for n in range(NCH):
                        ins = pe.transpose(side[1][:, n * P:(n + 1) * P], vn[:, c % 2, n * P:(n + 1) * P], ident)
                    ins.then_inc(vn_turned, 1)
                mix(3)
            loop(pe, span, body)
            pe.wait_ge(b_split, KT + 1)
            plainD("proj_b", (b_high, b_low))

            span = SPANS["gla"]

            def body(i):
                for hh in range(2):
                    h12, h2, h1 = i * 24 + 12 * hh, i * 4 + 2 * hh, i * 2 + hh
                    for c in range(6):
                        freeA(span, i, 6 * hh + c)
                        wblock(span, i, 6 * hh + c, U, accA[(span.a0 + 6 * hh + c) % 2])
                    pe.wait_ge(evacA, i * 12 + (span.a0 + 6 * hh + 3 + 3))
                    pe.wait_ge(o_rstd, i * 4 + (2 * hh + 1))
                    for n in range(NCH):
                        ins = pe.transpose(side[2][:, n * P:(n + 1) * P], R[:, 3, n * P:(n + 1) * P], ident)
                    ins.then_inc(v_turned, 1)
                    for n in range(12):
                        pe.wait_ge(x_pair, h12 + (n + 1))
                        pe.wait_ge(x_put, h12 + (n + 1))
                        d, lev = n // 6, n % 6
                        x = XL[:, n % 3]
                        for c in range(NCH):
                            cs = slice(c * P, (c + 1) * P)
                            if lev < 5:
                                h = LEVELS[lev]
                                q = x[:, cs].rearrange("p (b u t) -> p b u t", u=2, t=h)[:, :, 1 - d]
                                o = side[n % 2][:, c * P // 2:(c + 1) * P // 2].rearrange("p (b t) -> p b t", t=h)
                                ins = pe.matmul(o, x[:, cs], q, start=True, stop=True)
                            else:
                                key, query = (XL[:, 3], x) if d == 0 else (x, XL[:, 3])
                                ins = pe.matmul(side[n % 2][:, cs], key[:, cs], query[:, cs], start=True, stop=True)
                        ins.then_inc(x_mm, 1)
                    for d in range(2):
                        src = XL[:, 1] if d == 0 else XL[:, 2]
                        pe.wait_ge(e_mul, i * 8 + (4 * hh + 2 * d + 1 + 2))
                        if d == 0:
                            pe.wait_ge(v_taken, h1 + 1)
                        else:
                            pe.wait_ge(st_done, h2 + 1)
                        for n in range(NCH - 1):
                            c = n if d == 0 else n + 1
                            ins = pe.transpose(side[2][:, n * P:(n + 1) * P], src[:, c * P:(c + 1) * P], ident)
                        ins.then_inc(k_turned, 1)
                        pe.wait_ge(k_taken, h2 + (d + 1))
                        for n in range(NCH - 1):
                            c = n if d == 0 else n + 1
                            ins = pe.matmul(side[2][:, n * P:(n + 1) * P], k_tok[:, n], v_tok[:, c], start=True, stop=True)
                        ins.then_inc(st_mm, 1)
                    pe.wait_ge(x_put, h12 + 14)
                    pe.wait_ge(st_done, h2 + 2)
                    pe.wait_ge(e_mul, i * 8 + (4 * hh + 4 + 1))
                    for c in range(NCH):
                        cs = slice(c * P, (c + 1) * P)
                        o = side[3][:, cs]
                        pe.matmul(o, v_tok[:, c], att[:, 0, cs], start=True, stop=False)
                        ins = pe.matmul(o, v_tok[:, c], att[:, 1, cs], start=False, stop=False)
                        if c > 0:
                            ins = pe.matmul(o, Sd[:, 0, c - 1], XL[:, 0, cs], start=False, stop=c == NCH - 1)
                        if c < NCH - 1:
                            ins = pe.matmul(o, Sd[:, 1, c], XL[:, 3, cs], start=False, stop=True)
                    ins.then_inc(o_mm, 1)
                    pe.wait_ge(o_sq, h1 + 1)
                    pe.matmul(side[2][:], ones, head_s[:], start=True, stop=True).then_inc(o_stat, 1)
            pe.sem_inc(o_stat, 0) if False else None
            loop(pe, span, body)
            pe.wait_ge(ya_split, KT)
            plainD("proj_a", (ya_high, ya_low))
            pe.wait_ge(n_split, KT)
            plainD("w_out", (n_high, u_low))
            stat(4)

        @block.scalar
        def _(act):
            act.sem_inc(evacA, 2)
            act.sem_inc(s_exp, 4)
            act.sem_inc(o_rstd, 1)
            link = Chain(act, astep)

            def high(n, slot, turn):
                if isinstance(n, int) and n >= NBLK:
                    return
                act.wait_ge(landed[slot], 16 * turn + 16)
                act.wait_ge(block_done, n + 1)
                act.activation(w_high[:, slot], raw[:, slot], ACT.Copy).then_inc(hi_done, 1)

            def ahead(span, i, c):
                n = span.n0 + c + AHEAD
                high(blk(span, i, c + AHEAD), n % RING, i * (span.blocks // RING) + n // RING)

            def evac(span, i, c, t, out, func=ACT.Copy, **kw):
                act.wait_ge(block_done, blk(span, i, c) + (1 + RING))
                rows = kw.pop("rows", P)
                act.activation(out, accA[(span.a0 + t) % 2][0:rows], func, **kw).then_inc(evacA, 1)

            def norm_root(n, scale, bias):
                act.wait_ge(s_stat, n + 1)
                act.activation((root if n == 0 else root_late)[:], side[0][:], ACT.Sqrt, scale=scale, bias=bias).then_inc(s_root, 1)

            for n in range(AHEAD):
                high(n, n, 0)
            act.wait_ge(s_init, 1)
            norm_root(0, 1.0 / D, eps[:, 0:1])

            span = SPANS["conv_a"]

            def body(i):
                for c in range(span.blocks):
                    j = c // 3
                    ahead(span, i, c)
                    act.wait_ge(a_used, i * 4 + (j + 1))
                    evac(span, i, c, c, stage[:, j % 2, c % 3])
            loop(act, span, body)

            span = SPANS["dt"]
            ahead(span, 0, 0)
            act.wait_ge(s_par, 16)
            evac(span, 0, 0, 0, dtw[:, 3], ACT.Identity, bias=par[0:HEADS, PCOL["dt_bias"]:PCOL["dt_bias"] + 1], rows=HEADS)
            act.wait_ge(evacA, 2 + span.a0 + 1)
            link(act.activation(dtw[:, 4], dtw[:, 3], ACT.Abs))
            link(act.activation(dtw[:, 4], dtw[:, 4], ACT.Exp, scale=-1.0))
            act.activation(dtw[:, 4], dtw[:, 4], ACT.Ln, bias=1.0).then_inc(d_ln, 1)
            act.activation(dsmall[:, 0, 0:1], par[0:HEADS, PCOL["a_log"]:PCOL["a_log"] + 1], ACT.Exp).then_inc(d_ln, 1)
            act.wait_ge(d_acum, 1)
            act.activation(dtw[:, 2], dtw[:, 2], ACT.Exp).then_inc(d_exp, 1)
            act.activation(dsmall[:, 0, 4:8], dtw[:, 1, P - 1::P], ACT.Exp).then_inc(d_exp, 1)

            span = SPANS["gate_a"]

            def body(i):
                for c in range(span.blocks):
                    ahead(span, i, c)
                    evac(span, i, c, c, one(M, i * 4 + c), ACT.Sigmoid)
            loop(act, span, body)

            span = SPANS["w_a_out"]

            def body(i):
                for c in range(span.blocks):
                    ahead(span, i, c)
            loop(act, span, body)

            span = SPANS["ssd"]

            def body(i):
                for gg in range(2):
                    r10, e0 = i * 20 + 10 * gg, i * 12 + 6 * gg

                    def silu(e):
                        act.wait_ge(c_ready, e0 + (e + 1))
                        t = (Bc[:], Cc[:], xs[:, 0], xs[:, 1], xs[:, 0], xs[:, 1])[e]
                        act.activation(t, t, ACT.Silu).then_inc(c_silu, 1)

                    def head(h):
                        hh = i * 16 + (8 * gg + h)
                        act.wait_ge(s_seg, hh + 1)
                        act.wait_ge(s_y, hh + 1)
                        act.activation(cexp[:, h % 2], side[h % 2][:], ACT.Exp).then_inc(s_exp, 1)
                        act.wait_ge(s_min, hh + 1)
                        act.activation(seg[:, h % 2], seg[:, h % 2], ACT.Exp).then_inc(s_exp, 1)

                    for c in range(10):
                        ahead(span, i, 10 * gg + c)
                        if 1 <= c <= 6:
                            silu(c - 1)
                        act.wait_ge(c_used, r10 + (c + 1))
                        evac(span, i, 10 * gg + c, 10 * gg + c, raw_x[:, c % 2], ACT.Copy if c < 6 else ACT.Silu)
                        if c >= 6:
                            head(2 * (c - 6))
                            head(2 * (c - 6) + 1)
            loop(act, span, body)

            span = SPANS["gate_s"]
            for g in range(GROUPS):
                act.wait_ge(g_stat, g + 1)
                act.activation(groot[:, g], side[g][:], ACT.Sqrt, scale=1.0 / (D_INNER // GROUPS),
                               bias=eps[:, 0:1]).then_inc(g_root, 1)

            def body(i):
                for c in range(span.blocks):
                    ahead(span, i, c)
                    evac(span, i, c, c, one(sig_s, i * 4 + c), ACT.Sigmoid)
            loop(act, span, body)
            def only_ahead(name):
                span = SPANS[name]

                def body(i):
                    for c in range(span.blocks):
                        ahead(span, i, c)
                loop(act, span, body)

            only_ahead("w_s_out")
            only_ahead("w_o")

            norm_root(1, 1.0 / D, eps[:, 0:1])
            span = SPANS["w_up"]

            def body(i):
                for c in range(span.blocks):
                    ahead(span, i, c)
                    j = c // 2
                    if c % 2 == 0:
                        act.wait_ge(f_used, i * 4 + (2 * j + 1))
                        evac(span, i, c, c, h1_raw[:])
                    else:
                        act.wait_ge(f_conv, i * 2 + (j + 1))
                        act.activation(h1_conv[:], h1_conv[:], ACT.Silu).then_inc(f_silu, 1)
                        act.wait_ge(f_used, i * 4 + (2 * j + 2))
                        evac(span, i, c, c, h3_raw[:])
            loop(act, span, body)
            only_ahead("w_down")
            norm_root(2, 1.0 / D, eps[:, 0:1])
            norm_root(3, 1.0 / D, eps[:, 1:2])

            act.wait_ge(lb_v, 1)
            act.activation(lbc[:, 1], lbc[:, 1], ACT.Exp).then_inc(lb_a, 1)
            act.wait_ge(lb_v, 2)
            act.activation(lbc[:, 1], lbc[:, 1], ACT.Ln).then_inc(lb_a, 1)
            act.activation(lbc[:, 2], lbc[:, 2], ACT.Ln).then_inc(lb_a, 1)

            def evac_all(name, out, func):
                span = SPANS[name]

                def body(i):
                    for c in range(span.blocks):
                        ahead(span, i, c)
                        evac(span, i, c, c, one(out, i * span.blocks + c), func)
                loop(act, span, body)

            evac_all("sg_v", VG, ACT.Gelu_apprx_tanh)
            act.wait_ge(v_mean, 1)
            act.activation(ln_a[:], side[0][:], ACT.Copy, scale=1.0 / D).then_inc(v_mu, 1)
            evac_all("sg_u", UG, ACT.Gelu_apprx_tanh)
            act.wait_ge(v_var, 1)
            act.activation(ln_a[:], side[0][:], ACT.Sqrt, scale=1.0 / D, bias=eps[:, 2:3]).then_inc(v_root, 1)
            span = SPANS["sg_gb"]

            def body(i):
                for c in range(span.blocks):
                    ahead(span, i, c)
                    act.wait_ge(gs_used, i * 4 + (c + 1))
                    evac(span, i, c, c, vn[:, c % 2], ACT.Silu)
            loop(act, span, body)
            evac_all("mb", M2, ACT.Sigmoid)
            only_ahead("proj_b")

            span = SPANS["gla"]
            lcol = lambda k, d, i, hh: (lbc[:, k, bass.ds(i * 2 + (d * KT + hh), 1)] if not isinstance(i, int)
                                        else lbc[:, k, i * 2 + d * KT + hh:i * 2 + d * KT + hh + 1])

            def body(i):
                for hh in range(2):
                    h2, h5 = i * 4 + 2 * hh, i * 10 + 5 * hh
                    h12 = i * 24 + 12 * hh
                    for c in range(6):
                        ahead(span, i, 6 * hh + c)
                        if c < 5:
                            act.wait_ge(r_used, h5 + (c + 1))
                            evac(span, i, 6 * hh + c, 6 * hh + c, R[:, c], ACT.Silu if c in (2, 4) else ACT.Copy)
                        else:
                            evac(span, i, 6 * hh + c, 6 * hh + c, one(SA, i * 2 + hh), ACT.Sigmoid)
                        if c == 1:
                            for d in range(2):
                                act.wait_ge(evacA, i * 12 + (span.a0 + 6 * hh + d + 3))
                                if d == 0:
                                    act.wait_ge(e_mul, i * 8 + (4 * hh + 1))
                                link(act.activation(G[:, d], R[:, d], ACT.Abs))
                                link(act.activation(G[:, d], G[:, d], ACT.Exp, scale=-1.0))
                                act.activation(G[:, d], G[:, d], ACT.Ln, bias=1.0).then_inc(l_ln, 1)
                            for d in range(2):
                                act.wait_ge(l_k, h2 + (d + 1))
                                act.activation(Kd[:, d], Kd[:, d], ACT.Exp, bias=lcol(1, d, i, hh)).then_inc(l_floor, 1)
                                link(act.activation(XL[:, d], G[:, d], ACT.Abs, bias=lcol(4, d, i, hh)))
                                link(act.activation(XL[:, d], XL[:, d], ACT.Exp, scale=-1.0))
                                act.activation(XL[:, d], XL[:, d], ACT.Ln, bias=1.0).then_inc(l_floor, 1)
                    for n in range(12):
                        act.wait_ge(x_diff, h12 + (n + 1))
                        x = XL[:, n % 3]
                        if n % 6 == 5:
                            link(act.activation(XL[:, 3], x, ACT.Exp, scale=-1.0))
                        act.activation(x, x, ACT.Exp).then_inc(x_exp, 1)
                    for d in range(2):
                        act.wait_ge(e_diff, h2 + (d + 1))
                        act.activation(dtot[:, d], tot[:, d], ACT.Exp).then_inc(e_exp, 1)
                        act.activation(XL[:, 2 * d], G[:, d], ACT.Exp).then_inc(e_exp, 1)
                        act.activation(XL[:, 2 * d + 1], XL[:, 2 * d + 1], ACT.Exp).then_inc(e_exp, 1)
                    act.wait_ge(o_stat, i * 2 + (hh + 1))
                    act.activation(head_s[:], side[2][:], ACT.Ln, scale=1.0 / P, bias=eps[:, 1:2]).then_inc(o_rstd, 1)
                    act.wait_ge(o_rstd, i * 4 + (2 * hh + 2))
                    act.activation(head_s[:], head_s[:], ACT.Exp, scale=-0.5).then_inc(o_rstd, 1)
            loop(act, span, body, link, 20)
            only_ahead("proj_a")
            only_ahead("w_out")
            norm_root(4, 1.0 / D, eps[:, 1:2])

        @block.vector
        def _(dve):
            dve.sem_inc(evacD, 2)
            dve.sem_inc(a_used, 2)
            dve.sem_inc(c_used, 2)
            dve.sem_inc(s_taken, 1)
            dve.sem_inc(s_ytaken, 1)
            link = Chain(dve, vstep)
            tt, stt, ts, cp = dve.tensor_tensor, dve.scalar_tensor_tensor, dve.tensor_scalar, dve.tensor_copy

            def low(n, slot):
                if isinstance(n, int) and n >= NBLK:
                    return
                dve.wait_ge(hi_done, n + 1)
                tt(w_low[:, slot], raw[:, slot], w_high[:, slot].bitcast(F32), ALU.subtract).then_inc(lo_done, 1)

            def ahead(span, i, c):
                low(blk(span, i, c + AHEAD), (span.n0 + c + AHEAD) % RING)

            def split(value, high, lowp, done):
                link(cp(high, value))
                tt(lowp, value, high.bitcast(F32), ALU.subtract).then_inc(done, 1)

            def causal(out, x, taps, bias=None):
                if bias is None:
                    link(ts(out, x, taps[-1], None, ALU.mult))
                else:
                    link(ts(out, x, taps[-1], bias, ALU.mult, ALU.add))
                for s in range(1, len(taps)):
                    ins = stt(out[:, s:], x[:, :T - s], taps[-1 - s], out[:, s:], ALU.mult, ALU.add)
                    if s < len(taps) - 1:
                        link(ins)
                return ins

            link(dve.memset(eps[:, 0:1], EPS))
            link(dve.memset(eps[:, 1:2], RMS_EPS))
            dve.memset(eps[:, 2:3], LN_EPS).then_inc(s_init, 1)
            for n in range(AHEAD):
                low(n, n)
            dve.wait_ge(s_cst, 32)
            link(cp(identR[:], ident))
            link(cp(masks[:], masks_f[:]))
            dve.wait_ge(s_x, 16)
            link(tt(sums[:], X[:, 0], X[:, 0], ALU.mult))
            for k in range(1, KT):
                link(tt(norm_t[:], X[:, k], X[:, k], ALU.mult))
                ins = tt(sums[:], sums[:], norm_t[:], ALU.add)
                if k < KT - 1:
                    link(ins)
            ins.then_inc(s_sq, 1)

            def normed(n, weight, src, high, lowp):
                dve.wait_ge(s_root, n + 1)
                link(dve.reciprocal(rstd[:], root[:]))
                for k in range(KT):
                    link(stt(norm_t[:], src[:, k], col(weight, k), rstd[:], ALU.mult, ALU.mult))
                    split(norm_t[:], high[:, k], lowp[:, k], s_split)
                    dve.wait_ge(s_split, n * KT + k + 1)

            dve.wait_ge(s_par, 16)
            normed(0, "norm_mix_w", X, u_high, u_low)

            span = SPANS["conv_a"]

            def body(i):
                for c in range(span.blocks):
                    j = c // 3
                    ahead(span, i, c)
                    st = stage[:, j % 2]
                    if c % 3 == 1:
                        dve.wait_ge(evacA, i * 12 + (span.a0 + 3 + c))
                        link(tt(conv_p[:], st[:, 0], st[:, 1], ALU.mult))
                        link(causal(conv_o[:], conv_p[:], [col("conv_a_w", i * 4 + (k * KT + j)) for k in range(3)]))
                    if c % 3 == 2:
                        dve.wait_ge(evacA, i * 12 + (span.a0 + 3 + c))
                        dve.wait_ge(a_used, i * 4 + (j + 2))
                        tt(conv_o[:], conv_o[:], st[:, 2], ALU.mult).then_inc(a_used, 1)
                        dve.wait_ge(a_used, i * 4 + (j + 3))
                        split(conv_o[:], one(a_high, i * 4 + j), one(a_low, i * 4 + j), a_split)
                        dve.wait_ge(a_split, i * 4 + (j + 1))
            loop(dve, span, body, link, 20)

            span = SPANS["dt"]
            ahead(span, 0, 0)
            dve.wait_ge(d_ln, 2)
            dt, acum, dec = dtw[:, 0], dtw[:, 1], dtw[:, 2]
            link(stt(dt, dtw[:, 3], 0.0, dtw[:, 4], ALU.max, ALU.add))
            link(ts(dtw[:, 5], dt, dsmall[:, 0, 0:1], -1.0, ALU.mult, ALU.mult))
            link(dve.memset(dtw[:, 6], 1.0))
            link(dve.memset(dtw[:, 6, 0::P], 0.0))
            link(dve.tensor_tensor_scan(acum, dtw[:, 6], dtw[:, 5], 0.0, ALU.mult, ALU.add))
            a4 = acum.rearrange("h (c t) -> h c t", t=P)
            tt(dec.rearrange("h (c t) -> h c t", t=P), a4[:, :, P - 1:P].to_broadcast([HEADS, NCH, P]), a4,
               ALU.subtract).then_inc(d_acum, 1)
            link(cp(acum_high[:], acum))
            link(tt(acum_low[:], acum, acum_high[:].bitcast(F32), ALU.subtract))
            dve.wait_ge(d_exp, 2)
            link(tt(dec, dec, dt, ALU.mult))
            tt(dsmall[:, 1].rearrange("h (c k) -> h c k", c=NCH),
               cst[0:HEADS, 0:1, 0:HEADS].to_broadcast([HEADS, NCH, HEADS]),
               dsmall[:, 0, 4:8].rearrange("h (c o) -> h c o", o=1).to_broadcast([HEADS, NCH, HEADS]), ALU.mult).then_inc(d_done, 1)

            span = SPANS["gate_a"]

            def body(i):
                for c in range(span.blocks):
                    ahead(span, i, c)
            loop(dve, span, body)
            dve.wait_ge(d_turned, 1)
            link(cp(tok[:].rearrange("p a c h -> p (a c h)"), side[0][:, 0:3 * NCH * HEADS]))
            cp(decay_b[:].rearrange("p c h -> p (c h)"), side[1][:, 0:NCH * HEADS]).then_inc(d_tok, 1)

            span = SPANS["w_a_out"]

            def body(i):
                for c in range(span.blocks):
                    ahead(span, i, c)
                    dve.wait_ge(block_done, blk(span, i, c) + (1 + RING))
                    m = one(M, i * 4 + c)
                    dve.wait_ge(evacA, 2 + span.a0)
                    tt(m, m, accD[(span.d0 + c) % 2][:], ALU.mult).then_inc(evacD, 1)
            loop(dve, span, body)

            span = SPANS["ssd"]
            dve.wait_ge(d_tok, 1)

            def body(i):
                for gg in range(2):
                    r10, r8, r4, r1 = i * 20 + 10 * gg, i * 16 + 8 * gg, i * 8 + 4 * gg, i * 2 + gg
                    g = r1
                    taken = [0]

                    def conv(e):
                        xt = g + (2 * KT if e == 0 else 2 * KT + GROUPS) if e < 2 else r4 + (e - 2)
                        out = (Bc[:], Cc[:], xs[:, 0], xs[:, 1], xs[:, 0], xs[:, 1])[e]
                        dve.wait_ge(evacA, i * 20 + (span.a0 + 10 * gg + e + 3))
                        taps = [col("ssd_conv_w", xt + k * (D_XBC // P)) for k in range(4)]
                        link(causal(out, raw_x[:, e % 2], taps, col("ssd_conv_b", xt)))
                        dve.nop().then_inc(c_used, 1) if False else None
                        dve.sem_inc(c_used, 1)
                        dve.sem_inc(c_ready, 1)

                    def took(ins):
                        ins.then_inc(s_taken, 1)
                        taken[0] += 1
                        dve.wait_ge(s_taken, r8 + (taken[0] + 1))

                    def turned():
                        dve.wait_ge(s_turned, r8 + (taken[0] + 1))

                    def take_x(j):
                        dve.wait_ge(c_silu, i * 12 + (6 * gg + 2 + j + 1))
                        link(ts(one(Y, r4 + j), xs[:, j % 2], col("d_skip", r4 + j), None, ALU.mult))
                        turned()
                        src = side[3][:].rearrange("p (c h d) -> p c h d", c=NCH, d=HEAD_DIM)
                        for which, dst, n in ((2, xdec, NCH - 1), (0, xdt, NCH)):
                            for c in range(n):
                                h0 = r8 + 2 * j
                                w = tok[:, which, c, bass.ds(h0, 2)] if not isinstance(h0, int) else tok[:, which, c, h0:h0 + 2]
                                ins = tt(dst[:, c, j * P:(j + 1) * P].rearrange("p (h d) -> p h d", d=HEAD_DIM),
                                         src[:, c], w.rearrange("p (h o) -> p h o", o=1).to_broadcast([P, 2, HEAD_DIM]), ALU.mult)
                                if which == 2 and c == n - 1:
                                    ins.then_inc(s_scaled, 1)
                        took(ins)

                    def head(h):
                        hh = i * 16 + (8 * gg + h)
                        dve.wait_ge(s_exp, i * 32 + (16 * gg + 2 * h + 1 + 4))
                        dve.wait_ge(s_y, hh + 1)
                        for c in range(NCH):
                            cs = slice(c * P, (c + 1) * P)
                            k = c * HEADS + (r8 + h)
                            a_s = tok[:, 1, c, bass.ds(r8 + h, 1)] if not isinstance(r8, int) else tok[:, 1, c, r8 + h:r8 + h + 1]
                            ins = ts(seg[:, h % 2, cs], side[h % 2][:, cs], a_s, 0.0, ALU.subtract, ALU.min)
                        ins.then_inc(s_min, 1)
                        tt(cexp[:, h % 2], cexp[:, h % 2], Cc[:], ALU.mult).then_inc(s_mat, 1)
                        dve.wait_ge(s_exp, i * 32 + (16 * gg + 2 * h + 2 + 4))
                        tt(seg[:, h % 2], seg[:, h % 2], CBm[:].rearrange("p c t -> p (c t)"), ALU.mult).then_inc(s_mat, 1)

                    def take_y(j):
                        dve.wait_ge(s_y, i * 16 + (8 * gg + 2 * j + 1 + 3))
                        y = one(Y, r4 + j)
                        tt(y, y, side[2][:], ALU.add).then_inc(s_ytaken, 1)
                        dve.wait_ge(s_ytaken, r4 + (j + 2))
                        dve.wait_ge(evacA, i * 20 + (span.a0 + 10 * gg + 6 + j + 3))
                        z = raw_x[:, j % 2]
                        link(tt(y, y, z, ALU.mult))
                        link(tt(z, y, y, ALU.mult))
                        gs = one(gsum, g)
                        if j == 0:
                            ins = cp(gs, z)
                        else:
                            ins = tt(gs, gs, z, ALU.add)
                        ins.then_inc(c_used, 1)
                        dve.wait_ge(c_used, r10 + (6 + j + 3))

                    for c in range(10):
                        ahead(span, i, 10 * gg + c)
                        if c == 0:
                            dve.wait_ge(s_y, r8 + 2)
                            gl = r8 if isinstance(r8, int) else None
                            src = identR[0:HEADS, r8:r8 + 8] if gl is not None else identR[0:HEADS, bass.ds(r8, 8)]
                            cp(pick[:, gg], src.bitcast(F32)).then_inc(s_pick, 1)
                        if 4 <= c <= 6:
                            take_x(c - 4)
                        if c < 6:
                            conv(c)
                        if c == 2:
                            turned()
                            took(cp(Btok[:].rearrange("p c t -> p (c t)"), side[3][:]))
                            dve.wait_ge(s_cb, r1 + 1)
                            link(tt(CBm[:], side[2][:].rearrange("p (c t) -> p c t", c=NCH),
                                    cst[:, 2:3].to_broadcast([P, NCH, P]), ALU.mult))
                        if c == 6:
                            take_x(3)
                            for k in range(NCH - 1):
                                turned()
                                st = xdec[:, k]
                                if k == 0:
                                    took(cp(st, side[3][:]))
                                    continue
                                h0 = r8
                                w = decay_b[:, k, bass.ds(h0, 8)] if not isinstance(h0, int) else decay_b[:, k, h0:h0 + 8]
                                link(tt(st.rearrange("p (h d) -> p h d", d=HEAD_DIM),
                                        xdec[:, k - 1].rearrange("p (h d) -> p h d", d=HEAD_DIM),
                                        w.rearrange("p (h o) -> p h o", o=1).to_broadcast([P, 8, HEAD_DIM]), ALU.mult))
                                took(tt(st, st, side[3][:], ALU.add))
                        if c >= 6:
                            head(2 * (c - 6))
                            head(2 * (c - 6) + 1)
                            if c >= 7:
                                take_y(c - 7)
                    take_y(3)
                    dve.sem_inc(g_sq, 1)
            loop(dve, span, body, link, 78)

            span = SPANS["gate_s"]

            def body(i):
                for c in range(span.blocks):
                    ahead(span, i, c)
                    g = i * 2 + c // 2
                    if c % 2 == 0:
                        dve.wait_ge(g_root, g + 1)
                        link(dve.reciprocal(one(groot, g), one(groot, g)))
                    for k in (2 * (c % 2), 2 * (c % 2) + 1):
                        y = one(Y, i * 8 + 4 * (c // 2) + k)
                        link(stt(y, y, col("ssd_norm_w", i * 8 + 4 * (c // 2) + k), one(groot, g), ALU.mult, ALU.mult))
            loop(dve, span, body, link, 10)

            span = SPANS["w_s_out"]
            dve.wait_ge(block_done, span.n0 + RING)
            for k in range(2 * KT):
                split(Y[:, k], y_high[:, k], y_low[:, k], y_split)
            dve.wait_ge(y_split, 2 * KT)

            def body(i):
                for c in range(span.blocks):
                    ahead(span, i, c)
                    if c % 2:
                        j = i * 2 + c // 2
                        dve.wait_ge(block_done, blk(span, i, c) + (1 + RING))
                        tt(sums[:], one(sig_s, j), accD[(span.d0 + c // 2) % 2][:], ALU.mult).then_inc(evacD, 1)
                        dve.wait_ge(evacD, i * 2 + (span.d0 + c // 2 + 3))
                        link(tt(one(M, j), one(M, j), sums[:], ALU.add))
                        split(one(M, j), one(m_high, j), one(m_low, j), m_split)
                        dve.wait_ge(m_split, j + 1)
            loop(dve, span, body, link, 4)

            def residual(name, square):
                span = SPANS[name]
                per = span.blocks // span.dtiles

                def body(i):
                    for c in range(span.blocks):
                        ahead(span, i, c)
                        if c % per == per - 1:
                            t = c // per
                            j = i * span.dtiles + t
                            x = one(X, j)
                            dve.wait_ge(block_done, blk(span, i, c) + (1 + RING))
                            tt(x, x, accD[(span.d0 + t) % 2][:], ALU.add).then_inc(evacD, 1)
                            dve.wait_ge(evacD, i * span.dtiles + (span.d0 + t + 3))
                            link(tt(square[:], x, x, ALU.mult))
                            link(tt(sums[:], sums[:], square[:], ALU.add))
                link(dve.memset(sums[:], 0.0))
                loop(dve, span, body, link, 2 * span.dtiles)
                dve.sem_inc(s_sq, 1)

            residual("w_o", norm_t)

            def normed_late(n, weight, done, outs=None):
                dve.wait_ge(s_root, n + 1)
                link(dve.reciprocal(root_late[:], root_late[:]))
                for k in range(KT):
                    if outs is None:
                        link(stt(X[:, k], X[:, k], col(weight, k), root_late[:], ALU.mult, ALU.mult))
                    else:
                        link(stt(norm_e[:], X[:, k], col(weight, k), root_late[:], ALU.mult, ALU.mult))
                        split(norm_e[:], outs[0][:, k], outs[1][:, k], s_split)
                        dve.wait_ge(s_split, done + k + 1)

            normed_late(1, "norm_ffn_w", KT, (u_high, u_low))

            span = SPANS["w_up"]
            dve.sem_inc(f_used, 2)

            def body(i):
                for c in range(span.blocks):
                    ahead(span, i, c)
                    j = i * 2 + c // 2
                    dve.wait_ge(evacA, i * 4 + (span.a0 + c + 3))
                    if c % 2 == 0:
                        taps = [col("ffn_conv_w", i * 2 + (k * FT + c // 2)) for k in range(3)]
                        link(causal(h1_conv[:], h1_raw[:], taps, col("ffn_conv_b", j)))
                        dve.sem_inc(f_conv, 1)
                        dve.sem_inc(f_used, 1)
                    else:
                        dve.wait_ge(f_silu, j + 1)
                        tt(h1_conv[:], h1_conv[:], h3_raw[:], ALU.mult).then_inc(f_used, 1)
                        dve.wait_ge(f_used, i * 4 + (2 * (c // 2) + 4))
                        split(h1_conv[:], one(f_high, j), one(f_low, j), f_split)
                        dve.wait_ge(f_split, j + 1)
            loop(dve, span, body, link, 8)
            residual("w_down", norm_f)
            normed_late(2, "final_norm_w", 0)
            link(tt(sums[:], X[:, 0], X[:, 0], ALU.mult))
            for k in range(1, KT):
                link(tt(norm_e[:], X[:, k], X[:, k], ALU.mult))
                link(tt(sums[:], sums[:], norm_e[:], ALU.add))
            dve.sem_inc(s_sq, 1)
            normed_late(3, "norm_w_2", 2 * KT, (u_high, u_low))

            lbr = par[:, PCOL["lower_bounds_2"]:PCOL["lower_bounds_2"] + 2 * KT]
            tt(lbc[:, 1], lbr, lbr, ALU.subtract).then_inc(lb_v, 1)
            dve.wait_ge(lb_a, 1)
            link(dve.reciprocal(lbc[:, 2], lbc[:, 1]))
            link(tt(lbc[:, 1], lbc[:, 1], lbc[:, 2], ALU.mult))
            link(tt(lbc[:, 0], lbc[:, 1], lbc[:, 1], ALU.subtract))
            link(ts(lbc[:, 1], lbc[:, 0], -1.0, 1.0, ALU.mult, ALU.add))
            ts(lbc[:, 2], lbc[:, 0], LB_FLOOR, 2.0 ** 40, ALU.max, ALU.mult).then_inc(lb_v, 1)
            dve.wait_ge(lb_a, 3)
            link(ts(lbc[:, 2], lbc[:, 2], -40.0 * float(np.log(2.0)), None, ALU.add))
            link(tt(lbc[:, 3], lbc[:, 2], lbc[:, 1], ALU.subtract))
            link(tt(lbc[:, 4], lbc[:, 1], lbc[:, 2], ALU.subtract))

            span = SPANS["sg_v"]
            link(dve.memset(sums[:], 0.0))

            def body(i):
                for c in range(span.blocks):
                    ahead(span, i, c)
                    dve.wait_ge(evacA, i * 4 + (span.a0 + c + 3))
                    link(tt(sums[:], sums[:], one(VG, i * 4 + c), ALU.add))
            loop(dve, span, body, link, 4)
            dve.sem_inc(v_sum, 1)
            dve.wait_ge(v_mu, 1)
            link(dve.memset(sums[:], 0.0))
            span = SPANS["sg_u"]

            def body(i):
                for c in range(span.blocks):
                    ahead(span, i, c)
                    v = one(VG, i * 4 + c)
                    link(tt(v, v, ln_a[:], ALU.subtract))
                    link(tt(ln_b[:], v, v, ALU.mult))
                    link(tt(sums[:], sums[:], ln_b[:], ALU.add))
            loop(dve, span, body, link, 12)
            dve.sem_inc(v_sq, 1)
            dve.wait_ge(v_root, 1)
            link(dve.reciprocal(ln_a[:], ln_a[:]))
            span = SPANS["sg_gb"]
            dve.sem_inc(gs_used, 2)

            def body(i):
                for c in range(span.blocks):
                    ahead(span, i, c)
                    v, u = one(VG, i * 4 + c), one(UG, i * 4 + c)
                    link(stt(v, v, col("ln_w_2", i * 4 + c), ln_a[:], ALU.mult, ALU.mult))
                    dve.wait_ge(evacA, i * 4 + (span.a0 + c + 3))
                    tt(u, u, vn[:, c % 2], ALU.mult).then_inc(gs_used, 1)
                    dve.wait_ge(gs_used, i * 4 + (c + 3))
            loop(dve, span, body, link, 4)

            span = SPANS["mb"]
            dve.sem_inc(b_split, 1)

            def body(i):
                def finish(c):
                    j = i * 4 + c
                    dve.wait_ge(s_mix, j + 1)
                    link(tt(ln_b[:], one(UG, j), side[2][:], ALU.mult))
                    split(ln_b[:], one(b_high, j), one(b_low, j), b_split)
                    dve.wait_ge(b_split, j + 2)

                for c in range(span.blocks):
                    ahead(span, i, c)
                    j = i * 4 + c
                    ts(vn[:, c % 2], one(VG, j), col("ln_b_2", j), None, ALU.add).then_inc(vn_done, 1)
                    if c:
                        finish(c - 1)
                    dve.wait_ge(vn_turned, j + 1)
                    cp(vt[:, c % 2].rearrange("p c t -> p (c t)"), side[1][:]).then_inc(vt_done, 1)
                finish(3)
            loop(dve, span, body, link, 8)

            def scale(name, dst):
                span = SPANS[name]

                def body(i):
                    for c in range(span.blocks):
                        ahead(span, i, c)
                        m = one(dst, i * 4 + c)
                        dve.wait_ge(block_done, blk(span, i, c) + (1 + RING))
                        tt(m, m, accD[(span.d0 + c) % 2][:], ALU.mult).then_inc(evacD, 1)
                loop(dve, span, body)

            dve.wait_ge(evacA, 2 + SPANS["gla"].a0)
            scale("proj_b", M2)

            span = SPANS["gla"]
            link(dve.memset(att[:], 0.0))
            link(dve.memset(resets[:], 1.0))
            link(dve.memset(resets[:, 0::P], 0.0))
            dve.sem_inc(r_used, 5)
            dve.sem_inc(x_put, 2)
            dve.sem_inc(e_mul, 1)
            dve.sem_inc(o_rstd, 0) if False else None

            def gcol(k, d, i, hh):
                n = i * 2 + (d * KT + hh)
                return lbc[:, k, n:n + 1] if isinstance(n, int) else lbc[:, k, bass.ds(n, 1)]

            def body(i):
                for hh in range(2):
                    h12, h2, h1, h5 = i * 24 + 12 * hh, i * 4 + 2 * hh, i * 2 + hh, i * 10 + 5 * hh
                    for c in range(6):
                        ahead(span, i, 6 * hh + c)
                        if c == 1:
                            for d in range(2):
                                dve.wait_ge(l_ln, h2 + (d + 1))
                                link(stt(G[:, d], R[:, d], 0.0, G[:, d], ALU.min, ALU.subtract))
                                if d == 0:
                                    link(tt(Kd[:, d], G[:, d], R[:, d], ALU.subtract))
                                else:
                                    link(tt(Kd[:, d], G[:, d], R[:, d], ALU.subtract))
                                dve.sem_inc(r_used, 1)
                                dve.sem_inc(l_k, 1)
                        if c == 2:
                            for d in range(2):
                                dve.wait_ge(l_floor, i * 8 + (4 * hh + 2 * d + 2))
                                link(stt(XL[:, d], G[:, d], gcol(3, d, i, hh), XL[:, d], ALU.max, ALU.add))
                                link(ts(XL[:, d], XL[:, d], gcol(1, d, i, hh), None, ALU.add))
                                link(dve.tensor_tensor_scan(G[:, d], resets[:], XL[:, d], 0.0, ALU.mult, ALU.add))
                                link(cp(tot[:, d], G[:, d, P - 1::P]))
                                if d == 1:
                                    link(tt(G[:, 1], G[:, 1], XL[:, 1], ALU.subtract))
                            dve.wait_ge(evacA, i * 12 + (span.a0 + 6 * hh + 2 + 3))
                            link(ts(R[:, 2], R[:, 2], float(P) ** -0.5, None, ALU.mult))
                    dve.wait_ge(v_turned, h1 + 1)
                    cp(v_tok[:].rearrange("p c t -> p (c t)"), side[2][:]).then_inc(v_taken, 1)
                    Q = R[:, 2]

                    def halves(t, h):
                        return t.rearrange("p (b u t) -> p b u t", u=2, t=h)

                    def diff(n):
                        d, lev = n // 6, n % 6
                        g, x = G[:, d], XL[:, n % 3]
                        if n >= 3:
                            dve.wait_ge(x_mm, h12 + (n - 2))
                        if lev < 5:
                            h = LEVELS[lev]
                            gh, xh = halves(g, h), halves(x, h)
                            ref = (gh[:, :, 0, h - 1:h] if d == 0 else gh[:, :, 1, 0:1]).to_broadcast([P, T // (2 * h), h])
                            tt(xh[:, :, 0], ref, gh[:, :, 0], ALU.subtract)
                            tt(xh[:, :, 1], gh[:, :, 1], ref, ALU.subtract).then_inc(x_diff, 1)
                        else:
                            gb = g.rearrange("p (b t) -> p b t", t=BOTTOM)
                            link(tt(rsum[:], gb[:, :, 1], gb[:, :, 2], ALU.add))
                            stt(x.rearrange("p (b t) -> p b t", t=BOTTOM),
                                rsum[:].rearrange("p (b o) -> p b o", o=1).to_broadcast([P, T // BOTTOM, BOTTOM]),
                                -0.5, gb, ALU.mult, ALU.add).then_inc(x_diff, 1)

                    def pair(n):
                        d, lev = n // 6, n % 6
                        x, key = XL[:, n % 3], Kd[:, d]
                        dve.wait_ge(x_exp, h12 + (n + 1))
                        if lev < 5:
                            h = LEVELS[lev]
                            xh = halves(x, h)
                            a, b = (key, Q) if d == 0 else (Q, key)
                            tt(xh[:, :, 0], xh[:, :, 0], halves(a, h)[:, :, 0], ALU.mult)
                            tt(xh[:, :, 1], xh[:, :, 1], halves(b, h)[:, :, 1], ALU.mult).then_inc(x_pair, 1)
                        else:
                            tt(x, x, Q if d == 0 else key, ALU.mult)
                            tt(XL[:, 3], XL[:, 3], key if d == 0 else Q, ALU.mult).then_inc(x_pair, 1)

                    def put(n):
                        d, lev = n // 6, n % 6
                        dve.wait_ge(x_mm, h12 + (n + 1))
                        dve.wait_ge(x_put, h12 + (n + 2))
                        dve.sem_inc(x_clear, 1)
                        at = sum(T // 2 for _ in range(lev))
                        size = T // 2 if lev < 5 else T
                        mask = masks[:, d, at:at + size]
                        if lev < 5:
                            h = LEVELS[lev]
                            a = halves(att[:, d], h)[:, :, 1 - d]
                            data = side[n % 2][:, 0:size].rearrange("p (b t) -> p b t", t=h)
                            mask = mask.rearrange("p (b t) -> p b t", t=h)
                        else:
                            a, data = att[:, d], side[n % 2][:]
                        dve.copy_predicated(a, mask, data).then_inc(x_put, 1)

                    diff(0)
                    for n in range(12):
                        if n + 1 < 12:
                            diff(n + 1)
                        pair(n)
                        if n:
                            put(n - 1)
                    put(11)
                    for d in range(2):
                        gt = G[:, d].rearrange("p (c t) -> p c t", t=P)
                        tt(XL[:, 2 * d + 1].rearrange("p (c t) -> p c t", t=P),
                           tot[:, d].rearrange("p (c o) -> p c o", o=1).to_broadcast([P, NCH, P]), gt,
                           ALU.subtract).then_inc(e_diff, 1)
                    for d in range(2):
                        a, b = (Q, Kd[:, 0]) if d == 0 else (Kd[:, 1], Q)
                        dve.wait_ge(e_exp, i * 12 + (6 * hh + 3 * d + 3))
                        tt(XL[:, 2 * d], XL[:, 2 * d], a, ALU.mult).then_inc(e_mul, 1)
                        tt(XL[:, 2 * d + 1], XL[:, 2 * d + 1], b, ALU.mult).then_inc(e_mul, 1)
                    dve.sem_inc(r_used, 2) if False else None
                    for d in range(2):
                        dve.wait_ge(k_turned, h2 + (d + 1))
                        cp(k_tok[:].rearrange("p c t -> p (c t)"), side[2][:, 0:(NCH - 1) * P]).then_inc(k_taken, 1)
                        dve.wait_ge(st_mm, h2 + (d + 1))
                        order = (0, 1, 2) if d == 0 else (2, 1, 0)
                        for k, n in enumerate(order):
                            st = side[2][:, n * P:(n + 1) * P]
                            if k == 0:
                                ins = cp(Sd[:, d, n], st)
                            else:
                                c = n if d == 0 else n + 1
                                ins = stt(Sd[:, d, n], Sd[:, d, order[k - 1]], dtot[:, d, c:c + 1], st, ALU.mult, ALU.add)
                            if k < 2:
                                link(ins)
                        ins.then_inc(st_done, 1)
                    dve.wait_ge(o_mm, h1 + 1)
                    link(cp(head_o[:], side[3][:]))
                    tt(head_s[:], head_o[:], head_o[:], ALU.mult).then_inc(o_sq, 1)
                    dve.wait_ge(o_rstd, i * 4 + (2 * hh + 3))
                    link(stt(head_o[:], head_o[:], col("gnorm_w_2", 0), head_s[:], ALU.mult, ALU.mult))
                    dve.wait_ge(evacA, i * 12 + (span.a0 + 6 * hh + 4 + 3))
                    link(tt(one(Ya, h1), head_o[:], R[:, 4], ALU.mult))
                    dve.sem_inc(r_used, 3)
            loop(dve, span, body, link, 46)

            for k in range(KT):
                split(Ya[:, k], ya_high[:, k], ya_low[:, k], ya_split)
            dve.wait_ge(ya_split, KT)
            span = SPANS["proj_a"]

            def body(i):
                for c in range(span.blocks):
                    ahead(span, i, c)
                    j = i * 4 + c
                    dve.wait_ge(block_done, blk(span, i, c) + (1 + RING))
                    tt(sums[:], one(SA, j), accD[(span.d0 + c) % 2][:], ALU.mult).then_inc(evacD, 1)
                    dve.wait_ge(evacD, i * 4 + (span.d0 + c + 3))
                    link(tt(sums[:], sums[:], one(M2, j), ALU.add))
                    split(sums[:], one(n_high, j), one(u_low, j), n_split)
                    dve.wait_ge(n_split, j + 1)
            loop(dve, span, body, link, 8)
            residual("w_out", norm_e)
            normed_late(4, "final_norm_w_2", 0)
            dve.sem_inc(s_fin, 1)

        @block.gpsimd
        def _(pool):
            pool.wait_ge(v_sum, 1)
            pool.dma_start(ws_t[:], ws_in).then_inc(s_ws, 16)
            pool.dma_start(bs_row[:], bs_in).then_inc(s_ws, 16)
            pool.wait_ge(s_fin, 1)
            pool.dma_start(out.rearrange("(k p) t -> p k t", p=P), X[:]).then_inc(s_out, 16)
            pool.wait_ge(s_out, 16)


def cols(v, n):
    return np.asarray(v).reshape(-1, P).T


def consts():
    i = np.arange(P)
    return np.stack([np.eye(P), np.ones((P, P)), i[:, None] <= i[None, :]], 1).astype(np.float32)


def level_masks():
    t = np.arange(T) % P
    s = np.arange(P)[:, None]
    out = []
    for back in range(2):
        row = []
        for h in LEVELS:
            half = (t // h) % 2 == (0 if back else 1)
            q = t[half][None, :]
            row.append(s // (2 * h) == q // (2 * h))
            row[-1] = row[-1] & ((s // h) % 2 == (1 if back else 0))
        q = t[None, :]
        row.append((s // BOTTOM == q // BOTTOM) & ((s >= q) if back else (s <= q)))
        out.append(np.concatenate(row, 1))
    return np.stack(out, 1).astype(np.float32)


def weight_stream(w):
    def blocks(m, columns, rows=None):
        rows = np.arange(KT * P) if rows is None else rows
        return [m[rows][:, columns].reshape(KT, P, P).transpose(1, 0, 2)]

    def cut(m, start, j, k0=0):
        return [m[k0 * P:(k0 + KT) * P, start + j * P:start + (j + 1) * P].reshape(KT, P, P).transpose(1, 0, 2)]

    w_in, out = w["w_in"][0], []
    for j in range(KT):
        for at in (C_A, V_A, B_A):
            out += cut(w_in, at, j)
    out += blocks(w_in, list(range(DT, DT + HEADS)) + list(range(DT - P + HEADS, DT)))
    for j in range(KT):
        out += cut(w_in, GATE_A, j)
    for j in range(KT):
        out += cut(w["w_a_out"][0], 0, j)
    for g in range(GROUPS):
        out += cut(w_in, XBC + D_INNER, g) + cut(w_in, XBC + D_INNER + GROUPS * D_STATE, g)
        for at in (XBC, Z):
            for j in range(4):
                out += cut(w_in, at, 4 * g + j)
    for j in range(KT):
        out += cut(w_in, GATE_S, j)
    for j in range(KT):
        out += cut(w["w_s_out"][0], 0, j) + cut(w["w_s_out"][0], 0, j, KT)
    for j in range(KT):
        out += cut(w["w_o"][0], 0, j)
    for j in range(FT):
        out += cut(w["w_up"][0], 0, j) + cut(w["w_up"][0], D_FF, j)
    for j in range(KT):
        out += cut(w["w_down"][0], 0, j) + cut(w["w_down"][0], 0, j, KT) + cut(w["w_down"][0], 0, j, FT - KT)
    w2 = w["w_in_2"][0]
    for at in (V2, U2, GB2, MB2):
        for j in range(KT):
            out += cut(w2, at, j)
    for j in range(KT):
        out += cut(w["w_proj_b_2"][0], 0, j)
    for j in range(KT):
        for at in (FF2, FB2, Q2, I2, GA2, MA2):
            out += cut(w2, at, j)
    for name in ("w_proj_a_2", "w_out_2"):
        for j in range(KT):
            out += cut(w[name][0], 0, j)
    return out


def kernel(**inputs):
    import concourse.bacc as bacc
    from concourse.bass_utils import run_bass_kernel_spmd

    w = {k: np.asarray(v) for k, v in inputs.items()}
    stream = np.stack([b.reshape(P, KT * P) for b in weight_stream(w)[:NBLK]])
    pad = {k: np.zeros((P, 1), np.float32) for k in ("dt_bias", "a_log")}
    columns = []
    for name, n in PARAMS:
        v = w[name]
        if name in pad:
            pad[name][:HEADS, 0] = v[0]
            v = pad[name]
        elif name == "d_skip":
            v = cols(np.repeat(v[0], HEAD_DIM), n)
        else:
            v = cols(v, n)
        assert v.shape == (P, n), (name, v.shape)
        columns.append(v)
    arrays = {
        "x_t": np.ascontiguousarray(w["x"][0].T),
        "stream": stream,
        "params": np.ascontiguousarray(np.concatenate(columns, 1)),
        "consts": consts(),
        "masks": level_masks(),
        "spatial_w": np.ascontiguousarray(w["w_s_2"][0].transpose(2, 0, 1)),
        "spatial_b": np.ascontiguousarray(w["b_s_2"][0][None]),
    }
    nc = bacc.Bacc("TRN2", target_bir_lowering=False, num_devices=1)
    args = [nc.dram_tensor(k, a.shape, mybir.dt.from_np(a.dtype), kind="ExternalInput").ap() for k, a in arrays.items()]
    out = nc.dram_tensor("out_t", (D, T), F32, kind="ExternalOutput").ap()
    build(nc, *args, out)
    r = run_bass_kernel_spmd(nc, [arrays], core_ids=[0])
    return np.ascontiguousarray(np.asarray(r.results[0]["out_t"]).T)[None]
```

```python
from contextlib import ExitStack

import numpy as np

import concourse.bass as bass
from concourse import mybir

P = 128
T = 512
D = 1024
KT = D // P
D_INNER = 2 * D
HEADS = 32
HEAD_DIM = 64
GROUPS = 4
D_STATE = 128
D_XBC = D_INNER + 2 * GROUPS * D_STATE
D_FF = 2816
FT = D_FF // P
NCH = T // P
EPS = 1e-5
RMS_EPS = 1e-6
LN_EPS = 1e-5
LB_FLOOR = 1e-20
RING = 4
AHEAD = 2
LEVELS = (64, 32, 16, 8, 4)
BOTTOM = 4

F32 = mybir.dt.float32
F32R = mybir.dt.float32r
U8 = mybir.dt.uint8
ALU = mybir.AluOpType
ACT = mybir.ActivationFunctionType

GATE_A, GATE_S, B_A, C_A, V_A, Z, XBC = np.cumsum([0, D, D, D, D, D, D_INNER]).tolist()
DT = XBC + D_XBC
Q2, FF2, FB2, I2, GA2, U2, V2, GB2, MA2, MB2 = (D * k for k in range(10))

PARAMS = [
    ("norm_mix_w", KT), ("conv_a_w", 3 * KT), ("ssd_conv_w", 4 * D_XBC // P), ("ssd_conv_b", D_XBC // P),
    ("dt_bias", 1), ("a_log", 1), ("d_skip", D_INNER // P), ("ssd_norm_w", D_INNER // P),
    ("norm_ffn_w", KT), ("ffn_conv_w", 3 * FT), ("ffn_conv_b", FT), ("final_norm_w", KT),
    ("norm_w_2", KT), ("lower_bounds_2", 2 * KT), ("gnorm_w_2", 1), ("ln_w_2", KT), ("ln_b_2", KT),
    ("final_norm_w_2", KT),
]
PCOL = dict(zip([n for n, _ in PARAMS], np.cumsum([0] + [c for _, c in PARAMS]).tolist()))
NPAR = sum(c for _, c in PARAMS)

PHASES = [
    ("conv_a", 2, 12, 12, 0), ("dt", 1, 1, 1, 0), ("gate_a", 2, 4, 4, 0), ("w_a_out", 2, 4, 0, 4),
    ("ssd", 2, 20, 20, 0), ("gate_s", 2, 4, 4, 0), ("w_s_out", 4, 4, 0, 2), ("w_o", 2, 4, 0, 4),
    ("w_up", 11, 4, 4, 0), ("w_down", 2, 12, 0, 4),
    ("sg_v", 2, 4, 4, 0), ("sg_u", 2, 4, 4, 0), ("sg_gb", 2, 4, 4, 0), ("mb", 2, 4, 4, 0), ("proj_b", 2, 4, 0, 4),
    ("gla_first", 1, 4, 4, 0), ("gla", 4, 12, 12, 0), ("proj_a", 2, 4, 0, 4), ("w_out", 2, 4, 0, 4),
]


OWN = 2
PE_AT = {"start": [(0, 0, KT), (1, 0, KT)], 11: [(4, 0, 4)], "edge0": [(4, 4, KT)],
         "edge1": [(5, 0, 4)], "out": [(5, 4, KT)]}
for _n in range(8):
    PE_AT[_n] = [(2 + _n // 4, 2 * (_n % 4), 2 * (_n % 4) + 2)]
HI_AT = {"start": (0, 1), 0: (2,), 3: (3,), 7: (4,), 10: (5,)}
EVAC_AT = {0: (0,), 1: (1,), 5: (2,), 8: (3,), "edges": (4,), "out": (5,)}
LO_AT = {"start": (0, 1), 0: (2,), 3: (3,), 7: (4,), 10: (5,)}
GATE_ACT = {8: (0,), 9: (1,), "edges": (2, 3)}
GATE_DVE = {10: (0,), "out": (1,)}


def last_head(i, hh):
    return isinstance(i, int) and i * 2 + hh == KT - 1


class Span:

    def __init__(self, n0, a0, d0, phase):
        self.n0, self.a0, self.d0 = n0, a0, d0
        self.name, self.iters, self.blocks, self.atiles, self.dtiles = phase


def spans():
    out, n, a, d = {}, 0, 0, 0
    for ph in PHASES:
        out[ph[0]] = Span(n, a, d, ph)
        n, a, d = n + ph[1] * ph[2], a + ph[1] * ph[3], d + ph[1] * ph[4]
        if ph[0] == "gla":
            n, a = n - 4, a - 4
    return out, n


ROLLED = [name for name, iters, *_ in PHASES if iters > 1 and name != PHASES[-1][0]]
SPANS, NBLK = spans()


def build(nc, x_in, wall, par_in, consts_in, masks_in, ws_in, bs_in, out):
    ctx = ExitStack()
    with ctx:
        base = [-(-nc.sbuf_base // 64) * 64]

        def place(name, shape, dtype, at):
            return nc.alloc_sbuf_tensor_at(name, shape, dtype, offset=at)

        def fixed(name, shape, dtype):
            size = int(np.prod(shape[1:])) * (1 if dtype == U8 else 4)
            at = base[0]
            base[0] += -(-size // 64) * 64
            return place(name, shape, dtype, at)

        def sem(name):
            return ctx.enter_context(nc.semaphore(name))

        raw = fixed("raw", [P, RING, KT, P], F32)
        w_high = fixed("w_high", [P, RING, KT, P], F32R)
        w_low = fixed("w_low", [P, RING, KT, P], F32R)
        X = fixed("X", [P, KT, T], F32)
        act_at = base[0]
        u_high = fixed("u_high", [P, KT, T], F32R)
        u_low = fixed("u_low", [P, KT, T], F32R)
        par = fixed("par", [P, NPAR], F32)
        cst = fixed("cst", [P, 3, P], F32)
        ident, ones, upper = cst[:, 0], cst[:, 1], cst[:, 2]
        identR = fixed("identR", [P, P], F32R)
        masks = fixed("masks", [P, 2, len(LEVELS) * T // 2 + T], U8)
        tok = fixed("tok", [P, 3, NCH, HEADS], F32)
        decay_b = fixed("decay_b", [P, NCH, HEADS], F32)
        tok_end = base[0]
        acum_high = fixed("acum_high", [HEADS, T], F32R)
        acum_low = fixed("acum_low", [HEADS, T], F32R)
        ws_t = place("ws_t", [P, KT, P], F32, base[0] - 2 * 4 * T)
        pick = fixed("pick", [HEADS, 2, HEADS // GROUPS], F32R)
        lbc = fixed("lbc", [P, 6, 2 * KT], F32)
        eps = fixed("eps", [P, 4], F32)
        sums = fixed("sums", [P, T], F32)
        F = base[0]
        K = 1024

        def pcol(name, k=0):
            return par[:, PCOL[name] + k:PCOL[name] + k + 1]


        M = place("M", [P, KT, T], F32, F)
        masks_f = place("masks_f", [P, 2, len(LEVELS) * T // 2 + T], F32, F)
        a_high = place("a_high", [P, KT, T], F32R, F + 16 * K)
        a_low = place("a_low", [P, KT, T], F32R, F + 32 * K)
        Y = place("Y", [P, 2 * KT, T], F32, F + 16 * K)
        m_high = place("m_high", [P, KT, T], F32R, F + 16 * K)
        m_low = place("m_low", [P, KT, T], F32R, F + 32 * K)
        t0 = F + 48 * K
        stage = place("stage", [P, 2, 3, T], F32, t0)
        conv_p = place("conv_p", [P, T], F32, t0 + 12 * K)
        conv_o = place("conv_o", [P, T], F32, t0 + 14 * K)
        norm_t = place("norm_t", [P, T], F32, t0 + 16 * K)
        root = place("root", [P, T], F32, t0 + 18 * K)
        rstd = place("rstd", [P, T], F32, t0 + 20 * K)
        dtw = place("dtw", [HEADS, 8, T], F32, t0 + 22 * K)
        dsmall = place("dsmall", [HEADS, 2, NCH * HEADS], F32, t0 + 38 * K)
        raw_x = place("raw_x", [P, 2, T], F32, t0)
        Bc = place("Bc", [P, T], F32, t0 + 4 * K)
        Cc = place("Cc", [P, T], F32, t0 + 6 * K)
        Btok = place("Btok", [P, NCH, P], F32, t0 + 8 * K)
        CBm = place("CBm", [P, NCH, P], F32, t0 + 10 * K)
        xs = place("xs", [P, 2, T], F32, t0 + 12 * K)
        xdt = place("xdt", [P, NCH, T], F32, t0 + 16 * K)
        xdec = place("xdec", [P, NCH - 1, T], F32, t0 + 24 * K)
        seg = place("seg", [P, 2, T], F32, t0 + 30 * K)
        cexp = place("cexp", [P, 2, T], F32, t0 + 34 * K)
        gsum = place("gsum", [P, GROUPS, T], F32, t0 + 38 * K)
        sig_s = place("sig_s", [P, KT, T], F32, t0)
        groot = place("groot", [P, GROUPS, T], F32, t0 + 16 * K)
        y_high = place("y_high", [P, 2 * KT, T], F32R, t0 + 16 * K)
        y_low = place("y_low", [P, 2 * KT, T], F32R, act_at)

        f_high = place("f_high", [P, FT, T], F32R, F)
        f_low = place("f_low", [P, FT, T], F32R, F + 44 * K)
        h1_raw = place("h1_raw", [P, T], F32, F + 88 * K)
        h1_conv = place("h1_conv", [P, T], F32, F + 90 * K)
        h3_raw = place("h3_raw", [P, T], F32, F + 92 * K)
        root_late = place("root_late", [P, T], F32, F + 90 * K)
        norm_f = place("norm_f", [P, T], F32, F + 88 * K)
        squares = [norm_f, place("square_odd", [P, T], F32, F + 92 * K)]
        VG = place("VG", [P, KT, T], F32, F)
        UG = place("UG", [P, KT, T], F32, F + 16 * K)
        b_high = place("b_high", [P, KT, T], F32R, F + 32 * K)
        b_low = place("b_low", [P, KT, T], F32R, F + 48 * K)
        M2 = place("M2", [P, KT, T], F32, F + 64 * K)
        vn = place("vn", [P, 2, T], F32, F + 80 * K)
        vt = place("vt", [P, 2, NCH, P], F32, F + 84 * K)
        ln_a = place("ln_a", [P, T], F32, F + 88 * K)
        ln_b = place("ln_b", [P, T], F32, F + 90 * K)
        bs_row = place("bs_row", [1, KT, P], F32, F + 92 * K)
        Ya = place("Ya", [P, KT, T], F32, F)
        SA = place("SA", [P, KT, T], F32, F + 16 * K)
        R = place("R", [P, 5, T], F32, F + 32 * K)
        Kds = [place("Kd_even", [P, 2, T], F32, F + 42 * K), place("Kd_odd", [P, 2, T], F32, tok_end)]
        Gs = [place("G_even", [P, 2, T], F32, F + 46 * K), place("G_odd", [P, 2, T], F32, F + 92 * K)]
        extra = [sums, place("extra_back", [P, T], F32, tok_end - 4 * T)]
        v_tok = place("v_tok", [P, NCH, P], F32, F + 50 * K)
        att = place("att", [P, 2, T], F32, F + 52 * K)
        XL = place("XL", [P, 4, T], F32, F + 56 * K)
        Sd = place("Sd", [P, 2, NCH - 1, P], F32, F + 80 * K)
        k_tok = place("k_tok", [P, NCH - 1, P], F32, F + 83 * K)
        tots = place("tots", [P, 2, 2, NCH], F32, F + 84 * K + 512)
        dtot = place("dtot", [P, 2, NCH], F32, F + 84 * K + 576)
        rsum = place("rsum", [P, T // BOTTOM], F32, F + 84 * K + 1024)
        resets = place("resets", [P, T], F32, F + 86 * K)
        head_o = place("head_o", [P, T], F32, F + 88 * K)
        head_s = place("head_s", [P, T], F32, F + 90 * K)
        ya_high = place("ya_high", [P, KT, T], F32R, F + 32 * K)
        ya_low = place("ya_low", [P, KT, T], F32R, F + 48 * K)
        n_high = place("n_high", [P, KT, T], F32R, F)
        norm_e = place("norm_e", [P, T], F32, F + 88 * K)
        assert F + 96 * K <= nc.sbuf_usable_end, (F, nc.sbuf_usable_end)

        ps = [ctx.enter_context(nc.psum_tensor(f"bank{k}", [P, T], F32)) for k in range(8)]
        accA, accD, side = ps[0:2], ps[2:4], ps[4:8]

        landed = [sem(f"landed{s}") for s in range(RING)]
        hi_done, lo_done, block_done = sem("hi_done"), sem("lo_done"), sem("block_done")
        evacA, evacD = sem("evacA"), sem("evacD")
        s_par, s_cst, s_masks, s_out = sem("s_par"), sem("s_cst"), sem("s_masks"), sem("s_out")
        s_x = [sem(f"s_x{k}") for k in range(KT // 2)]
        vstep, astep = sem("vstep"), sem("astep")
        s_init, s_fin = sem("s_init"), sem("s_fin")
        s_sq, s_stat, s_root, s_split = sem("s_sq"), sem("s_stat"), sem("s_root"), sem("s_split")
        a_used, a_split = sem("a_used"), sem("a_split")
        d_ln, d_acum, d_exp, d_done, d_turned, d_tok = (
            sem(f"dt_{k}") for k in "ln acum exp done turned tok".split())
        c_ready, c_used, c_silu = sem("conv_ready"), sem("conv_used"), sem("conv_silu")
        s_turned, s_cb, s_taken = sem("ssd_turned"), sem("ssd_cb"), sem("ssd_taken")
        s_scaled, s_pick = sem("ssd_scaled"), sem("ssd_pick")
        s_seg, s_min, s_exp, s_mat, s_y, s_ytaken = (sem(f"ssd_{k}") for k in "seg min exp mat y ytaken".split())
        g_sq, g_stat, g_root, y_split, m_split = (sem(k) for k in "g_sq g_stat g_root y_split m_split".split())

        f_conv, f_silu, f_used, f_split = (sem(f"mlp_{k}") for k in "conv silu used split".split())
        s_ws = sem("s_ws")
        v_sum, v_mean, v_mu, v_sq, v_var, v_root = (sem(f"ln_{k}") for k in "sum mean mu sq var root".split())
        gs_used, vn_done, vn_turned, vt_done, s_mix, b_split = (
            sem(f"sg_{k}") for k in "gsused vn turned vt mix split".split())
        x_scaled, x_squared, x_summed = sem("x_scaled"), sem("x_squared"), sem("x_summed")
        x_clear = sem("hg_clear")
        lb_a, lb_v = sem("lb_a"), sem("lb_v")
        r_used, l_ln, l_k, l_floor, v_turned, v_taken = (
            sem(f"hg_{k}") for k in "used ln k floor vturned vtaken".split())
        x_diff, x_exp, x_pair, x_mm, x_put = (sem(f"hg_{k}") for k in "diff exp pair mm put".split())
        e_diff, e_exp, e_mul, k_turned, k_taken, st_mm, st_done = (
            sem(f"hg_{k}") for k in "ediff eexp emul kturned ktaken stmm stdone".split())
        o_mm, o_sq, o_stat, o_rstd, ya_split, n_split = (
            sem(k) for k in "o_mm o_sq o_stat o_rstd ya_split n_split".split())

        block = ctx.enter_context(nc.Block())

        class Chain:

            def __init__(self, eng, s):
                self.eng, self.s, self.base, self.per, self.i, self.k = eng, s, 0, 0, 0, 0

            def __call__(self, ins):
                self.k += 1
                ins.then_inc(self.s, 1)
                self.eng.wait_ge(self.s, self.i * self.per + (self.base + self.k))

        def loop(eng, span, body, chain=None, per=0):
            rolled = span.name in ROLLED
            if chain:
                chain.base, chain.k, chain.per = chain.base + chain.k, 0, per
            if rolled:
                last = span.name == "gla"
                with eng.Fori(0, span.iters - last) as i:
                    if chain:
                        chain.i = i
                    body(i)
                if last:
                    if chain:
                        assert chain.k == per, (span.name, chain.k, per)
                        chain.i, chain.k = span.iters - 1, 0
                    body(span.iters - 1)
                if chain:
                    assert last or chain.k == per, (span.name, chain.k, per)
                    chain.base, chain.k = chain.base + (span.iters - last) * per + (chain.k if last else 0), 0
            else:
                for i in range(span.iters):
                    body(i)
            if chain:
                chain.per = chain.i = 0

        def blk(span, i, c):
            return i * span.blocks + (span.n0 + c)

        def one(t, k):
            if isinstance(k, int):
                return t[:, k]
            return t[:, bass.ds(k, 1)].rearrange("p o t -> p (o t)")

        def col(name, k):
            if isinstance(k, int):
                return pcol(name, k)
            return par[:, bass.ds(k + PCOL[name], 1)]

        @block.sync
        def _(sp):
            for k in range(0, KT, 2):
                sp.dma_start(X[:, k:k + 2], x_in.rearrange("(k p) t -> p k t", p=P)[:, k:k + 2]).then_inc(s_x[k // 2], 16)
            sp.dma_start(cst[:], consts_in).then_inc(s_cst, 16)
            sp.dma_start(par[:], par_in).then_inc(s_par, 16)
            for n in range(RING):
                sp.dma_start(raw[:, n], wall[n].rearrange("p (k c) -> p k c", k=KT)).then_inc(landed[n], 16)
            sp.dma_start(masks_f[:], masks_in).then_inc(s_masks, 16)

            def load(n, s):
                sp.wait_ge(lo_done, n + (1 - RING))
                src = wall[n] if isinstance(n, int) else wall[bass.ds(n, 1)].rearrange("o p k -> (o p) k")
                sp.dma_start(raw[:, s], src.rearrange("p (k c) -> p k c", k=KT)).then_inc(landed[s], 16)

            with sp.Fori(1, NBLK // RING) as i:
                for s in range(RING):
                    load(i * RING + s, s)
            for n in range(NBLK // RING * RING, NBLK):
                load(n, n % RING)


        @block.tensor
        def _(pe):
            pe.sem_inc(block_done, RING)
            pe.sem_inc(s_y, 2)

            def wblock(span, i, c, moving, acc, kts=range(KT), at=0, start=True, stop=True, ready=None):
                xh, xl = moving
                slot = (span.n0 + c) % RING
                kts = list(kts)
                part = kts[-1] < KT - 1
                pe.wait_ge(lo_done, blk(span, i, c) + 1)
                for k in kts:
                    if ready:
                        pe.wait_ge(ready[0], ready[1] + k + 1)
                    for j, (w, x) in enumerate(((w_high, xh), (w_high, xl), (w_low, xh))):
                        ins = pe.matmul(acc[:], w[:, slot, k], x[:, at + k],
                                        start=start and k == kts[0] and j == 0,
                                        stop=stop and k == kts[-1] and j == 2)
                if not part:
                    ins.then_inc(block_done, 1)

            def freeA(span, i, t):
                pe.wait_ge(evacA, i * span.atiles + (span.a0 + t + 1))

            def freeD(span, i, t):
                pe.wait_ge(evacD, i * span.dtiles + (span.d0 + t + 1))

            def stat(n):
                pe.wait_ge(s_sq, n + 1)
                pe.matmul(side[0][:], ones, sums[:], start=True, stop=True).then_inc(s_stat, 1)

            def plainA(name, moving, ready=None):
                span = SPANS[name]

                def body(i):
                    for c in range(span.blocks):
                        freeA(span, i, c)
                        wblock(span, i, c, moving, accA[(span.a0 + c) % 2], ready=None if c else ready)
                loop(pe, span, body)

            def plainD(name, moving, ready=None):
                span = SPANS[name]

                def body(i):
                    for c in range(span.blocks):
                        freeD(span, i, c)
                        wblock(span, i, c, moving, accD[(span.d0 + c) % 2], ready=None if c else ready)
                loop(pe, span, body)

            U = (u_high, u_low)
            pe.wait_ge(s_cst, 16)
            stat(0)
            plainA("conv_a", U, (s_split, 0))
            plainA("dt", U)
            plainA("gate_a", U)
            pe.wait_ge(d_done, 1)
            for j in range(3):
                for c in range(NCH):
                    k = j * NCH + c
                    pe.transpose(side[0][:, k * HEADS:(k + 1) * HEADS], dtw[:, j, c * P:(c + 1) * P],
                                 cst[0:HEADS, 0, 0:HEADS])
            pe.matmul(side[1][:, 0:NCH * HEADS], cst[0:HEADS, 1], dsmall[:, 1],
                      start=True, stop=True).then_inc(d_turned, 1)
            pe.wait_ge(a_split, KT)
            plainD("w_a_out", (a_high, a_low))

            span = SPANS["ssd"]

            def ssd_group(i, gg):
                r8, r4, r1 = i * 16 + 8 * gg, i * 8 + 4 * gg, i * 2 + gg
                turned = [0]

                def mm(c):
                    freeA(span, i, 10 * gg + c)
                    wblock(span, i, 10 * gg + c, U, accA[(span.a0 + 10 * gg + c) % 2])

                def turn(src, silu):
                    pe.wait_ge(c_silu, i * 12 + (6 * gg + silu + 1))
                    pe.wait_ge(s_taken, r8 + (turned[0] + 1))
                    for c in range(NCH):
                        ins = pe.transpose(side[3][:, c * P:(c + 1) * P], src[:, c * P:(c + 1) * P], ident)
                    ins.then_inc(s_turned, 1)
                    turned[0] += 1

                def seg_rows(h):
                    pe.wait_ge(s_exp, i * 32 + (16 * gg + 2 * h + 2))
                    for n, part in enumerate((acum_high, acum_low)):
                        ins = pe.matmul(side[h % 2][:], pick[:, gg, h:h + 1].to_broadcast([HEADS, P]), part[:],
                                        start=n == 0, stop=n == 1)
                    ins.then_inc(s_seg, 1)

                def head_y(h):
                    rows = slice(HEAD_DIM * (h % 2), HEAD_DIM * (h % 2) + HEAD_DIM)
                    hs = slice(h * HEAD_DIM, (h + 1) * HEAD_DIM)
                    if h % 2 == 0:
                        pe.wait_ge(s_ytaken, r4 + (h // 2 + 1))
                    pe.wait_ge(s_mat, i * 32 + (16 * gg + 2 * h + 2))
                    for c in range(NCH):
                        cs = slice(c * P, (c + 1) * P)
                        ins = pe.matmul(side[2][rows, cs], xdt[:, c, hs], seg[:, h % 2, cs], start=True, stop=c == 0)
                        if c:
                            ins = pe.matmul(side[2][rows, cs], xdec[:, c - 1, hs], cexp[:, h % 2, cs],
                                            start=False, stop=True)
                    ins.then_inc(s_y, 1)

                for c in range(3):
                    mm(c)
                turn(Bc, 0)
                pe.wait_ge(c_silu, i * 12 + (6 * gg + 2))
                pe.wait_ge(s_ytaken, r4 + 1)
                for c in range(NCH):
                    cs = slice(c * P, (c + 1) * P)
                    ins = pe.matmul(side[2][:, cs], Bc[:, cs], Cc[:, cs], start=True, stop=True)
                ins.then_inc(s_cb, 1)
                for j in range(4):
                    mm(3 + j)
                    turn(xs[:, j % 2], 2 + j)
                pe.wait_ge(s_pick, r1 + 1)
                seg_rows(0)
                seg_rows(1)
                for c in range(NCH - 1):
                    pe.wait_ge(s_scaled, r4 + 4)
                    pe.wait_ge(s_taken, r8 + (turned[0] + 1))
                    pe.matmul(side[3][:], Btok[:, c], xdec[:, c], start=True, stop=True).then_inc(s_turned, 1)
                    turned[0] += 1
                for j in range(3):
                    mm(7 + j)
                    for h in (2 * j, 2 * j + 1):
                        head_y(h)
                    for h in (2 * j + 2, 2 * j + 3):
                        seg_rows(h)
                for h in (6, 7):
                    head_y(h)

            def body(i):
                for gg in range(2):
                    ssd_group(i, gg)
            loop(pe, span, body)

            for g in range(GROUPS):
                pe.wait_ge(g_sq, g + 1)
                if g == 0:
                    pe.wait_ge(g_sq, GROUPS)
                pe.matmul(side[g][:], ones, gsum[:, g], start=True, stop=True).then_inc(g_stat, 1)
            plainA("gate_s", U)
            span = SPANS["w_s_out"]

            def body(i):
                for t in range(2):
                    freeD(span, i, t)
                    for half in range(2):
                        wblock(span, i, 2 * t + half, (y_high, y_low), accD[(span.d0 + t) % 2],
                               at=half * KT, start=half == 0, stop=half == 1,
                               ready=None if t else (y_split, half * KT))
            loop(pe, span, body)
            plainD("w_o", (m_high, m_low), (m_split, 0))

            stat(1)
            plainA("w_up", U, (s_split, KT))
            span = SPANS["w_down"]

            def body(i):
                for t in range(4):
                    freeD(span, i, t)
                    for part in range(3):
                        wblock(span, i, 3 * t + part, (f_high, f_low), accD[(span.d0 + t) % 2],
                               kts=range(KT) if part < 2 else range(3 * KT - FT, KT),
                               at=part * KT if part < 2 else FT - KT, start=part == 0, stop=part == 2,
                               ready=None if t else (f_split, part * KT if part < 2 else FT - KT))
            loop(pe, span, body)
            stat(2)
            pe.wait_ge(s_root, 3)
            for k in range(KT):
                pe.wait_ge(x_squared, k + 1)
                ins = pe.matmul(side[0][:], ones, squares[k % 2][:], start=k == 0, stop=k == KT - 1)
                if k < KT - 1:
                    ins.then_inc(x_summed, 1)
            ins.then_inc(s_stat, 1)
            plainA("sg_v", U, (s_split, 2 * KT))
            pe.wait_ge(v_sum, 1)
            pe.matmul(side[0][:], ones, sums[:], start=True, stop=True).then_inc(v_mean, 1)
            plainA("sg_u", U)
            pe.wait_ge(v_sq, 1)
            pe.matmul(side[0][:], ones, sums[:], start=True, stop=True).then_inc(v_var, 1)
            plainA("sg_gb", U)

            span = SPANS["mb"]
            pe.wait_ge(s_ws, 32)

            def body(i):
                def mix(c):
                    j = i * 4 + c
                    pe.wait_ge(vt_done, j + 1)
                    pe.wait_ge(b_split, j + 1)
                    w = ws_t[:, j] if isinstance(j, int) else ws_t[:, bass.ds(j, 1)].rearrange("p o t -> p (o t)")
                    b = bs_row[:, j] if isinstance(j, int) else bs_row[:, bass.ds(j, 1)].rearrange("p o t -> p (o t)")
                    for n in range(NCH):
                        o = side[2][:, n * P:(n + 1) * P]
                        pe.matmul(o, vt[:, c % 2, n], w, start=True, stop=False)
                        ins = pe.matmul(o, cst[0:1, 1], b, start=False, stop=True)
                    ins.then_inc(s_mix, 1)

                for c in range(span.blocks):
                    freeA(span, i, c)
                    wblock(span, i, c, U, accA[(span.a0 + c) % 2])
                    if c:
                        mix(c - 1)
                    pe.wait_ge(vn_done, i * 4 + (c + 1))
                    if c:
                        pe.wait_ge(vt_done, i * 4 + c)
                    for n in range(NCH):
                        ins = pe.transpose(side[1][:, n * P:(n + 1) * P], vn[:, c % 2, n * P:(n + 1) * P], ident)
                    ins.then_inc(vn_turned, 1)
                mix(3)
            loop(pe, span, body)
            plainD("proj_b", (b_high, b_low), (b_split, 1))
            plainA("gla_first", U)

            span = SPANS["gla"]

            def body(i):
                for hh in range(2):
                    h12, h2, h1 = i * 24 + 12 * hh, i * 4 + 2 * hh, i * 2 + hh

                    def blocks_at(place):
                        for c, k0, k1 in PE_AT.get(place, ()):
                            if c < OWN or not last_head(i, hh):
                                if k0 == 0:
                                    freeA(span, i, 6 * hh + c)
                                wblock(span, i, 6 * hh + c, U, accA[(span.a0 + 6 * hh + c) % 2],
                                       kts=range(k0, k1), start=k0 == 0, stop=k1 == KT)

                    blocks_at("start")

                    def turn_values():
                        pe.wait_ge(evacA, i * 12 + (span.a0 + 6 * hh - 2 + 3))
                        pe.wait_ge(o_rstd, i * 4 + (2 * hh + 1))
                        for n in range(NCH):
                            ins = pe.transpose(side[2][:, n * P:(n + 1) * P], R[:, 3, n * P:(n + 1) * P], ident)
                        ins.then_inc(v_turned, 1)

                    for n in range(12):
                        pe.wait_ge(x_pair, h12 + (n + 1))
                        pe.wait_ge(x_put, h12 + (n + 1))
                        d, lev = n // 6, n % 6
                        x = XL[:, n % 3]
                        for c in range(NCH):
                            cs = slice(c * P, (c + 1) * P)
                            if lev < 5:
                                h = LEVELS[lev]
                                q = x[:, cs].rearrange("p (b u t) -> p b u t", u=2, t=h)[:, :, 1 - d]
                                o = side[n % 2][:, c * P // 2:(c + 1) * P // 2].rearrange("p (b t) -> p b t", t=h)
                                ins = pe.matmul(o, x[:, cs], q, start=True, stop=True)
                            else:
                                key, query = (XL[:, 3], x) if d == 0 else (x, XL[:, 3])
                                ins = pe.matmul(side[n % 2][:, cs], key[:, cs], query[:, cs], start=True, stop=True)
                        ins.then_inc(x_mm, 1)
                        blocks_at(n)
                        if n == 1:
                            turn_values()
                    for d in range(2):
                        src = XL[:, 1] if d == 0 else XL[:, 2]
                        pe.wait_ge(e_mul, i * 8 + (4 * hh + 2 * d + 1 + 2))
                        if d == 0:
                            pe.wait_ge(v_taken, h1 + 1)
                        else:
                            pe.wait_ge(st_done, h2 + 1)
                        for n in range(NCH - 1):
                            c = n if d == 0 else n + 1
                            ins = pe.transpose(side[2][:, n * P:(n + 1) * P], src[:, c * P:(c + 1) * P], ident)
                        ins.then_inc(k_turned, 1)
                        blocks_at("edge%d" % d)
                        pe.wait_ge(k_taken, h2 + (d + 1))
                        for n in range(NCH - 1):
                            c = n if d == 0 else n + 1
                            ins = pe.matmul(side[2][:, n * P:(n + 1) * P], k_tok[:, n], v_tok[:, c], start=True, stop=True)
                        ins.then_inc(st_mm, 1)
                    pe.wait_ge(x_put, h12 + 14)
                    pe.wait_ge(st_done, h2 + 2)
                    pe.wait_ge(e_mul, i * 8 + (4 * hh + 4 + 1))
                    for c in range(NCH):
                        cs = slice(c * P, (c + 1) * P)
                        o = side[3][:, cs]
                        pe.matmul(o, v_tok[:, c], att[:, 0, cs], start=True, stop=False)
                        ins = pe.matmul(o, v_tok[:, c], att[:, 1, cs], start=False, stop=False)
                        if c > 0:
                            ins = pe.matmul(o, Sd[:, 0, c - 1], XL[:, 0, cs], start=False, stop=c == NCH - 1)
                        if c < NCH - 1:
                            ins = pe.matmul(o, Sd[:, 1, c], XL[:, 3, cs], start=False, stop=True)
                    ins.then_inc(o_mm, 1)
                    blocks_at("out")
                    pe.wait_ge(o_sq, h1 + 1)
                    pe.matmul(side[2][:], ones, head_s[:], start=True, stop=True).then_inc(o_stat, 1)
            loop(pe, span, body)
            plainD("proj_a", (ya_high, ya_low), (ya_split, 0))
            plainD("w_out", (n_high, u_low), (n_split, 0))
            stat(3)

        @block.scalar
        def _(act):
            act.sem_inc(evacA, 2)
            act.sem_inc(s_exp, 4)
            act.sem_inc(o_rstd, 1)
            link = Chain(act, astep)

            def high(n, slot, turn):
                if isinstance(n, int) and n >= NBLK:
                    return
                act.wait_ge(landed[slot], 16 * turn + 16)
                act.wait_ge(block_done, n + 1)
                act.activation(w_high[:, slot], raw[:, slot], ACT.Copy).then_inc(hi_done, 1)

            def ahead(span, i, c):
                n = span.n0 + c + AHEAD
                high(blk(span, i, c + AHEAD), n % RING, i * (span.blocks // RING) + n // RING)

            def evac(span, i, c, t, out, func=ACT.Copy, **kw):
                act.wait_ge(block_done, blk(span, i, c) + (1 + RING))
                rows = kw.pop("rows", P)
                act.activation(out, accA[(span.a0 + t) % 2][0:rows], func, **kw).then_inc(evacA, 1)

            def norm_root(n, scale, bias):
                act.wait_ge(s_stat, n + 1)
                act.activation((root if n == 0 else root_late)[:], side[0][:], ACT.Sqrt, scale=scale, bias=bias).then_inc(s_root, 1)

            for n in range(AHEAD):
                high(n, n, 0)
            act.wait_ge(s_init, 1)
            norm_root(0, 1.0 / D, eps[:, 0:1])

            span = SPANS["conv_a"]

            def body(i):
                for c in range(span.blocks):
                    j = c // 3
                    ahead(span, i, c)
                    act.wait_ge(a_used, i * 4 + (j + 1))
                    evac(span, i, c, c, stage[:, j % 2, c % 3])
            loop(act, span, body)

            span = SPANS["dt"]
            ahead(span, 0, 0)
            act.wait_ge(s_par, 16)
            evac(span, 0, 0, 0, dtw[:, 3], ACT.Identity, bias=par[0:HEADS, PCOL["dt_bias"]:PCOL["dt_bias"] + 1], rows=HEADS)
            act.wait_ge(evacA, 2 + span.a0 + 1)
            link(act.activation(dtw[:, 4], dtw[:, 3], ACT.Abs))
            link(act.activation(dtw[:, 4], dtw[:, 4], ACT.Exp, scale=-1.0))
            act.activation(dtw[:, 4], dtw[:, 4], ACT.Ln, bias=1.0).then_inc(d_ln, 1)
            act.activation(dsmall[:, 0, 0:1], par[0:HEADS, PCOL["a_log"]:PCOL["a_log"] + 1], ACT.Exp).then_inc(d_ln, 1)
            act.wait_ge(d_acum, 1)
            act.activation(dtw[:, 2], dtw[:, 2], ACT.Exp).then_inc(d_exp, 1)
            act.activation(dsmall[:, 0, 4:8], dtw[:, 1, P - 1::P], ACT.Exp).then_inc(d_exp, 1)

            span = SPANS["gate_a"]

            def body(i):
                for c in range(span.blocks):
                    ahead(span, i, c)
                    evac(span, i, c, c, one(M, i * 4 + c), ACT.Sigmoid)
            loop(act, span, body)

            span = SPANS["w_a_out"]

            def body(i):
                for c in range(span.blocks):
                    ahead(span, i, c)
            loop(act, span, body)

            span = SPANS["ssd"]

            def body(i):
                for gg in range(2):
                    r10, e0 = i * 20 + 10 * gg, i * 12 + 6 * gg

                    def silu(e):
                        act.wait_ge(c_ready, e0 + (e + 1))
                        t = (Bc[:], Cc[:], xs[:, 0], xs[:, 1], xs[:, 0], xs[:, 1])[e]
                        act.activation(t, t, ACT.Silu).then_inc(c_silu, 1)

                    def head(h):
                        hh = i * 16 + (8 * gg + h)
                        act.wait_ge(s_seg, hh + 1)
                        act.wait_ge(s_y, hh + 1)
                        act.activation(cexp[:, h % 2], side[h % 2][:], ACT.Exp).then_inc(s_exp, 1)
                        act.wait_ge(s_min, hh + 1)
                        act.activation(seg[:, h % 2], seg[:, h % 2], ACT.Exp).then_inc(s_exp, 1)

                    for c in range(10):
                        ahead(span, i, 10 * gg + c)
                        if 1 <= c <= 6:
                            silu(c - 1)
                        act.wait_ge(c_used, r10 + (c + 1))
                        evac(span, i, 10 * gg + c, 10 * gg + c, raw_x[:, c % 2], ACT.Copy if c < 6 else ACT.Silu)
                        if c >= 6:
                            head(2 * (c - 6))
                            head(2 * (c - 6) + 1)
            loop(act, span, body)

            span = SPANS["gate_s"]
            for g in range(GROUPS):
                act.wait_ge(g_stat, g + 1)
                act.activation(groot[:, g], side[g][:], ACT.Sqrt, scale=1.0 / (D_INNER // GROUPS),
                               bias=eps[:, 0:1]).then_inc(g_root, 1)

            def body(i):
                for c in range(span.blocks):
                    ahead(span, i, c)
                    evac(span, i, c, c, one(sig_s, i * 4 + c), ACT.Sigmoid)
            loop(act, span, body)
            def only_ahead(name):
                span = SPANS[name]

                def body(i):
                    for c in range(span.blocks):
                        ahead(span, i, c)
                loop(act, span, body)

            only_ahead("w_s_out")
            only_ahead("w_o")

            norm_root(1, 1.0 / D, eps[:, 0:1])
            span = SPANS["w_up"]

            def body(i):
                for c in range(span.blocks):
                    ahead(span, i, c)
                    j = c // 2
                    if c % 2 == 0:
                        act.wait_ge(f_used, i * 4 + (2 * j + 1))
                        evac(span, i, c, c, h1_raw[:])
                    else:
                        act.wait_ge(f_conv, i * 2 + (j + 1))
                        act.activation(h1_conv[:], h1_conv[:], ACT.Silu).then_inc(f_silu, 1)
                        act.wait_ge(f_used, i * 4 + (2 * j + 2))
                        evac(span, i, c, c, h3_raw[:])
            loop(act, span, body)
            only_ahead("w_down")
            norm_root(2, 1.0 / D, eps[:, 0:1])
            for k in range(KT):
                act.wait_ge(x_scaled, k + 1)
                if k > 1:
                    act.wait_ge(x_summed, k - 1)
                act.activation(squares[k % 2][:], X[:, k], ACT.Square).then_inc(x_squared, 1)
            norm_root(3, 1.0 / D, eps[:, 1:2])

            act.wait_ge(lb_v, 1)
            act.activation(lbc[:, 1], lbc[:, 1], ACT.Exp).then_inc(lb_a, 1)
            act.wait_ge(lb_v, 2)
            act.activation(lbc[:, 1], lbc[:, 1], ACT.Ln).then_inc(lb_a, 1)
            act.activation(lbc[:, 2], lbc[:, 2], ACT.Ln).then_inc(lb_a, 1)

            def evac_all(name, out, func):
                span = SPANS[name]

                def body(i):
                    for c in range(span.blocks):
                        ahead(span, i, c)
                        evac(span, i, c, c, one(out, i * span.blocks + c), func)
                loop(act, span, body)

            evac_all("sg_v", VG, ACT.Gelu_apprx_tanh)
            act.wait_ge(v_mean, 1)
            act.activation(ln_a[:], side[0][:], ACT.Copy, scale=1.0 / D).then_inc(v_mu, 1)
            evac_all("sg_u", UG, ACT.Gelu_apprx_tanh)
            act.wait_ge(v_var, 1)
            act.activation(ln_a[:], side[0][:], ACT.Sqrt, scale=1.0 / D, bias=eps[:, 2:3]).then_inc(v_root, 1)
            span = SPANS["sg_gb"]

            def body(i):
                for c in range(span.blocks):
                    ahead(span, i, c)
                    act.wait_ge(gs_used, i * 4 + (c + 1))
                    evac(span, i, c, c, vn[:, c % 2], ACT.Silu)
            loop(act, span, body)
            evac_all("mb", M2, ACT.Sigmoid)
            only_ahead("proj_b")

            def act_gate(g2, col_at, odd, step):
                G, Kd = Gs[odd], Kds[odd]
                if step == 0:
                    for d in range(2):
                        link(act.activation(G[:, d], R[:, d], ACT.Abs))
                    for d in range(2):
                        link(act.activation(G[:, d], G[:, d], ACT.Exp, scale=-1.0))
                if step == 1:
                    for d in range(2):
                        act.activation(G[:, d], G[:, d], ACT.Ln, bias=1.0).then_inc(l_ln, 1)
                if step == 2:
                    for d in range(2):
                        act.wait_ge(l_k, g2 + (d + 1))
                        act.activation(Kd[:, d], Kd[:, d], ACT.Exp, bias=col_at(1, d)).then_inc(l_floor, 1)
                        link(act.activation(extra[d][:], G[:, d], ACT.Abs, bias=col_at(4, d)))
                        link(act.activation(extra[d][:], extra[d][:], ACT.Exp, scale=-1.0))
                if step == 3:
                    for d in range(2):
                        act.activation(extra[d][:], extra[d][:], ACT.Ln, bias=1.0).then_inc(l_floor, 1)

            span = SPANS["gla_first"]
            for c in range(4):
                ahead(span, 0, c)
                if c == 0:
                    act.wait_ge(r_used, 1)
                evac(span, 0, c, c, R[:, (0, 1, 3, 2)[c]], ACT.Silu if c == 3 else ACT.Copy)
            act.wait_ge(evacA, SPANS["gla"].a0)
            for step in range(4):
                act_gate(0, lambda k, d: lbc[:, k, d * KT:d * KT + 1], 0, step)

            span = SPANS["gla"]
            lcol = lambda k, d, i, hh: (lbc[:, k, bass.ds(i * 2 + (d * KT + hh), 1)] if not isinstance(i, int)
                                        else lbc[:, k, i * 2 + d * KT + hh:i * 2 + d * KT + hh + 1])

            def body(i):
                for hh in range(2):
                    h2 = i * 4 + 2 * hh
                    h12 = i * 24 + 12 * hh

                    def aheads_at(place):
                        for c in HI_AT.get(place, ()):
                            if c < OWN or not last_head(i, hh):
                                ahead(span, i, 6 * hh + c)

                    def evacs_at(place):
                        for c in EVAC_AT.get(place, ()):
                            if c >= OWN and last_head(i, hh):
                                continue
                            if c == 0:
                                act.wait_ge(r_used, i * 2 + (hh + 1))
                            elif c == 2 or c == 3:
                                act.wait_ge(l_k, h2 + (c - 1))
                            elif c == 4:
                                act.wait_ge(v_turned, i * 2 + (hh + 1))
                            elif c == 5:
                                act.wait_ge(e_mul, i * 8 + (4 * hh + 5))
                            dst = one(SA, i * 2 + hh) if c == 1 else R[:, (4, None, 0, 1, 3, 2)[c]]
                            func = (ACT.Silu, ACT.Sigmoid, ACT.Copy, ACT.Copy, ACT.Copy, ACT.Silu)[c]
                            evac(span, i, 6 * hh + c, 6 * hh + c, dst, func)

                    def gate_at(place):
                        for step in GATE_ACT.get(place, ()):
                            if last_head(i, hh):
                                continue
                            if step == 0:
                                act.wait_ge(evacA, i * 12 + (span.a0 + 6 * hh + 3 + 3))
                                act.wait_ge(e_mul, i * 8 + (4 * hh + 1))
                            act_gate(h2 + 2, lambda k, d: lcol(k, d, i, hh + 1), 1 - hh, step)

                    G, tot = Gs[hh], tots[:, hh]
                    aheads_at("start")
                    for n in range(12):
                        act.wait_ge(x_diff, h12 + (n + 1))
                        x = XL[:, n % 3]
                        if n % 6 == 5:
                            link(act.activation(XL[:, 3], x, ACT.Exp, scale=-1.0))
                        act.activation(x, x, ACT.Exp).then_inc(x_exp, 1)
                        aheads_at(n)
                        evacs_at(n)
                        gate_at(n)
                    for d in range(2):
                        act.wait_ge(e_diff, h2 + (d + 1))
                        act.activation(dtot[:, d], tot[:, d], ACT.Exp).then_inc(e_exp, 1)
                        act.activation(XL[:, 2 * d], G[:, d], ACT.Exp).then_inc(e_exp, 1)
                        act.activation(XL[:, 2 * d + 1], XL[:, 2 * d + 1], ACT.Exp).then_inc(e_exp, 1)
                    aheads_at("edges")
                    evacs_at("edges")
                    gate_at("edges")
                    act.wait_ge(o_stat, i * 2 + (hh + 1))
                    act.activation(head_s[:], side[2][:], ACT.Ln, scale=1.0 / P, bias=eps[:, 1:2]).then_inc(o_rstd, 1)
                    act.wait_ge(o_rstd, i * 4 + (2 * hh + 2))
                    act.activation(head_s[:], head_s[:], ACT.Exp, scale=-0.5).then_inc(o_rstd, 1)
                    evacs_at("out")
            loop(act, span, body, link, 20)
            only_ahead("proj_a")
            only_ahead("w_out")
            norm_root(4, 1.0 / D, eps[:, 1:2])

        @block.vector
        def _(dve):
            dve.sem_inc(evacD, 2)
            dve.sem_inc(a_used, 2)
            dve.sem_inc(c_used, 2)
            dve.sem_inc(s_taken, 1)
            dve.sem_inc(s_ytaken, 1)
            link = Chain(dve, vstep)
            tt, stt, ts, cp = dve.tensor_tensor, dve.scalar_tensor_tensor, dve.tensor_scalar, dve.tensor_copy

            def low(n, slot):
                if isinstance(n, int) and n >= NBLK:
                    return
                dve.wait_ge(hi_done, n + 1)
                tt(w_low[:, slot], raw[:, slot], w_high[:, slot].bitcast(F32), ALU.subtract).then_inc(lo_done, 1)

            def ahead(span, i, c):
                low(blk(span, i, c + AHEAD), (span.n0 + c + AHEAD) % RING)

            def split(value, high, lowp, done):
                link(cp(high, value))
                tt(lowp, value, high.bitcast(F32), ALU.subtract).then_inc(done, 1)

            def causal(out, x, taps, bias=None):
                if bias is None:
                    link(ts(out, x, taps[-1], None, ALU.mult))
                else:
                    link(ts(out, x, taps[-1], bias, ALU.mult, ALU.add))
                for s in range(1, len(taps)):
                    ins = stt(out[:, s:], x[:, :T - s], taps[-1 - s], out[:, s:], ALU.mult, ALU.add)
                    if s < len(taps) - 1:
                        link(ins)
                return ins

            link(dve.memset(eps[:, 0:1], EPS))
            link(dve.memset(eps[:, 1:2], RMS_EPS))
            dve.memset(eps[:, 2:3], LN_EPS).then_inc(s_init, 1)
            for k in range(KT):
                if k % 2 == 0:
                    dve.wait_ge(s_x[k // 2], 16)
                if k == 0:
                    link(tt(sums[:], X[:, 0], X[:, 0], ALU.mult))
                else:
                    link(tt(norm_t[:], X[:, k], X[:, k], ALU.mult))
                    ins = tt(sums[:], sums[:], norm_t[:], ALU.add)
                    if k < KT - 1:
                        link(ins)
            ins.then_inc(s_sq, 1)
            for n in range(AHEAD):
                low(n, n)

            def normed(n, weight, src, high, lowp):
                dve.wait_ge(s_root, n + 1)
                link(dve.reciprocal(rstd[:], root[:]))
                for k in range(KT):
                    link(stt(norm_t[:], src[:, k], col(weight, k), rstd[:], ALU.mult, ALU.mult))
                    split(norm_t[:], high[:, k], lowp[:, k], s_split)
                    dve.wait_ge(s_split, n * KT + k + 1)

            dve.wait_ge(s_par, 16)
            normed(0, "norm_mix_w", X, u_high, u_low)
            dve.wait_ge(s_cst, 16)
            link(cp(identR[:], ident))
            dve.wait_ge(s_masks, 16)
            link(cp(masks[:], masks_f[:]))

            span = SPANS["conv_a"]

            def body(i):
                for c in range(span.blocks):
                    j = c // 3
                    ahead(span, i, c)
                    st = stage[:, j % 2]
                    if c % 3 == 1:
                        dve.wait_ge(evacA, i * 12 + (span.a0 + 3 + c))
                        link(tt(conv_p[:], st[:, 0], st[:, 1], ALU.mult))
                        link(causal(conv_o[:], conv_p[:], [col("conv_a_w", i * 4 + (k * KT + j)) for k in range(3)]))
                    if c % 3 == 2:
                        dve.wait_ge(evacA, i * 12 + (span.a0 + 3 + c))
                        dve.wait_ge(a_used, i * 4 + (j + 2))
                        tt(conv_o[:], conv_o[:], st[:, 2], ALU.mult).then_inc(a_used, 1)
                        dve.wait_ge(a_used, i * 4 + (j + 3))
                        split(conv_o[:], one(a_high, i * 4 + j), one(a_low, i * 4 + j), a_split)
                        dve.wait_ge(a_split, i * 4 + (j + 1))
            loop(dve, span, body, link, 20)

            span = SPANS["dt"]
            ahead(span, 0, 0)
            dve.wait_ge(d_ln, 2)
            dt, acum, dec = dtw[:, 0], dtw[:, 1], dtw[:, 2]
            link(stt(dt, dtw[:, 3], 0.0, dtw[:, 4], ALU.max, ALU.add))
            link(ts(dtw[:, 5], dt, dsmall[:, 0, 0:1], -1.0, ALU.mult, ALU.mult))
            link(dve.memset(dtw[:, 6], 1.0))
            link(dve.memset(dtw[:, 6, 0::P], 0.0))
            link(dve.tensor_tensor_scan(acum, dtw[:, 6], dtw[:, 5], 0.0, ALU.mult, ALU.add))
            a4 = acum.rearrange("h (c t) -> h c t", t=P)
            tt(dec.rearrange("h (c t) -> h c t", t=P), a4[:, :, P - 1:P].to_broadcast([HEADS, NCH, P]), a4,
               ALU.subtract).then_inc(d_acum, 1)
            link(cp(acum_high[:], acum))
            link(tt(acum_low[:], acum, acum_high[:].bitcast(F32), ALU.subtract))
            dve.wait_ge(d_exp, 2)
            link(tt(dec, dec, dt, ALU.mult))
            tt(dsmall[:, 1].rearrange("h (c k) -> h c k", c=NCH),
               cst[0:HEADS, 0:1, 0:HEADS].to_broadcast([HEADS, NCH, HEADS]),
               dsmall[:, 0, 4:8].rearrange("h (c o) -> h c o", o=1).to_broadcast([HEADS, NCH, HEADS]), ALU.mult).then_inc(d_done, 1)

            span = SPANS["gate_a"]

            def body(i):
                for c in range(span.blocks):
                    ahead(span, i, c)
            loop(dve, span, body)
            dve.wait_ge(d_turned, 1)
            link(cp(tok[:].rearrange("p a c h -> p (a c h)"), side[0][:, 0:3 * NCH * HEADS]))
            cp(decay_b[:].rearrange("p c h -> p (c h)"), side[1][:, 0:NCH * HEADS]).then_inc(d_tok, 1)

            span = SPANS["w_a_out"]

            def body(i):
                for c in range(span.blocks):
                    ahead(span, i, c)
                    dve.wait_ge(block_done, blk(span, i, c) + (1 + RING))
                    m = one(M, i * 4 + c)
                    dve.wait_ge(evacA, 2 + span.a0)
                    tt(m, m, accD[(span.d0 + c) % 2][:], ALU.mult).then_inc(evacD, 1)
            loop(dve, span, body)

            span = SPANS["ssd"]
            dve.wait_ge(d_tok, 1)

            def body(i):
                for gg in range(2):
                    r10, r8, r4, r1 = i * 20 + 10 * gg, i * 16 + 8 * gg, i * 8 + 4 * gg, i * 2 + gg
                    g = r1
                    taken = [0]

                    def conv(e):
                        xt = g + (2 * KT if e == 0 else 2 * KT + GROUPS) if e < 2 else r4 + (e - 2)
                        out = (Bc[:], Cc[:], xs[:, 0], xs[:, 1], xs[:, 0], xs[:, 1])[e]
                        dve.wait_ge(evacA, i * 20 + (span.a0 + 10 * gg + e + 3))
                        taps = [col("ssd_conv_w", xt + k * (D_XBC // P)) for k in range(4)]
                        link(causal(out, raw_x[:, e % 2], taps, col("ssd_conv_b", xt)))
                        dve.sem_inc(c_used, 1)
                        dve.sem_inc(c_ready, 1)

                    def took(ins):
                        ins.then_inc(s_taken, 1)
                        taken[0] += 1
                        dve.wait_ge(s_taken, r8 + (taken[0] + 1))

                    def turned():
                        dve.wait_ge(s_turned, r8 + (taken[0] + 1))

                    def take_x(j):
                        dve.wait_ge(c_silu, i * 12 + (6 * gg + 2 + j + 1))
                        link(ts(one(Y, r4 + j), xs[:, j % 2], col("d_skip", r4 + j), None, ALU.mult))
                        turned()
                        src = side[3][:].rearrange("p (c h d) -> p c h d", c=NCH, d=HEAD_DIM)
                        for which, dst, n in ((2, xdec, NCH - 1), (0, xdt, NCH)):
                            for c in range(n):
                                h0 = r8 + 2 * j
                                w = tok[:, which, c, bass.ds(h0, 2)] if not isinstance(h0, int) else tok[:, which, c, h0:h0 + 2]
                                ins = tt(dst[:, c, j * P:(j + 1) * P].rearrange("p (h d) -> p h d", d=HEAD_DIM),
                                         src[:, c], w.rearrange("p (h o) -> p h o", o=1).to_broadcast([P, 2, HEAD_DIM]), ALU.mult)
                                if which == 2 and c == n - 1:
                                    ins.then_inc(s_scaled, 1)
                        took(ins)

                    def head(h):
                        hh = i * 16 + (8 * gg + h)
                        dve.wait_ge(s_exp, i * 32 + (16 * gg + 2 * h + 1 + 4))
                        dve.wait_ge(s_y, hh + 1)
                        for c in range(NCH):
                            cs = slice(c * P, (c + 1) * P)
                            a_s = tok[:, 1, c, bass.ds(r8 + h, 1)] if not isinstance(r8, int) else tok[:, 1, c, r8 + h:r8 + h + 1]
                            ins = ts(seg[:, h % 2, cs], side[h % 2][:, cs], a_s, 0.0, ALU.subtract, ALU.min)
                        ins.then_inc(s_min, 1)
                        tt(cexp[:, h % 2], cexp[:, h % 2], Cc[:], ALU.mult).then_inc(s_mat, 1)
                        dve.wait_ge(s_exp, i * 32 + (16 * gg + 2 * h + 2 + 4))
                        tt(seg[:, h % 2], seg[:, h % 2], CBm[:].rearrange("p c t -> p (c t)"), ALU.mult).then_inc(s_mat, 1)

                    def take_y(j):
                        dve.wait_ge(s_y, i * 16 + (8 * gg + 2 * j + 1 + 3))
                        y = one(Y, r4 + j)
                        tt(y, y, side[2][:], ALU.add).then_inc(s_ytaken, 1)
                        dve.wait_ge(s_ytaken, r4 + (j + 2))
                        dve.wait_ge(evacA, i * 20 + (span.a0 + 10 * gg + 6 + j + 3))
                        z = raw_x[:, j % 2]
                        link(tt(y, y, z, ALU.mult))
                        link(tt(z, y, y, ALU.mult))
                        gs = one(gsum, g)
                        if j == 0:
                            ins = cp(gs, z)
                        else:
                            ins = tt(gs, gs, z, ALU.add)
                        ins.then_inc(c_used, 1)
                        dve.wait_ge(c_used, r10 + (6 + j + 3))

                    for c in range(10):
                        ahead(span, i, 10 * gg + c)
                        if c == 0:
                            dve.wait_ge(s_y, r8 + 2)
                            src = identR[0:HEADS, r8:r8 + 8] if isinstance(r8, int) else identR[0:HEADS, bass.ds(r8, 8)]
                            cp(pick[:, gg], src.bitcast(F32)).then_inc(s_pick, 1)
                        if 4 <= c <= 6:
                            take_x(c - 4)
                        if c < 6:
                            conv(c)
                        if c == 2:
                            turned()
                            took(cp(Btok[:].rearrange("p c t -> p (c t)"), side[3][:]))
                            dve.wait_ge(s_cb, r1 + 1)
                            link(tt(CBm[:], side[2][:].rearrange("p (c t) -> p c t", c=NCH),
                                    cst[:, 2:3].to_broadcast([P, NCH, P]), ALU.mult))
                        if c == 6:
                            take_x(3)
                            for k in range(NCH - 1):
                                turned()
                                st = xdec[:, k]
                                if k == 0:
                                    took(cp(st, side[3][:]))
                                    continue
                                h0 = r8
                                w = decay_b[:, k, bass.ds(h0, 8)] if not isinstance(h0, int) else decay_b[:, k, h0:h0 + 8]
                                link(tt(st.rearrange("p (h d) -> p h d", d=HEAD_DIM),
                                        xdec[:, k - 1].rearrange("p (h d) -> p h d", d=HEAD_DIM),
                                        w.rearrange("p (h o) -> p h o", o=1).to_broadcast([P, 8, HEAD_DIM]), ALU.mult))
                                took(tt(st, st, side[3][:], ALU.add))
                        if c >= 6:
                            head(2 * (c - 6))
                            head(2 * (c - 6) + 1)
                            if c >= 7:
                                take_y(c - 7)
                    take_y(3)
                    dve.sem_inc(g_sq, 1)
            loop(dve, span, body, link, 78)

            span = SPANS["gate_s"]

            def body(i):
                for c in range(span.blocks):
                    ahead(span, i, c)
                    g = i * 2 + c // 2
                    if c % 2 == 0:
                        dve.wait_ge(g_root, g + 1)
                        link(dve.reciprocal(one(groot, g), one(groot, g)))
                    for k in (2 * (c % 2), 2 * (c % 2) + 1):
                        y = one(Y, i * 8 + 4 * (c // 2) + k)
                        link(stt(y, y, col("ssd_norm_w", i * 8 + 4 * (c // 2) + k), one(groot, g), ALU.mult, ALU.mult))
            loop(dve, span, body, link, 10)

            span = SPANS["w_s_out"]
            dve.wait_ge(block_done, span.n0 + RING)
            for k in range(2 * KT):
                split(Y[:, k], y_high[:, k], y_low[:, k], y_split)
            dve.wait_ge(y_split, 2 * KT)

            def body(i):
                for c in range(span.blocks):
                    ahead(span, i, c)
                    if c % 2:
                        j = i * 2 + c // 2
                        dve.wait_ge(block_done, blk(span, i, c) + (1 + RING))
                        tt(sums[:], one(sig_s, j), accD[(span.d0 + c // 2) % 2][:], ALU.mult).then_inc(evacD, 1)
                        dve.wait_ge(evacD, i * 2 + (span.d0 + c // 2 + 3))
                        link(tt(one(M, j), one(M, j), sums[:], ALU.add))
                        split(one(M, j), one(m_high, j), one(m_low, j), m_split)
                        dve.wait_ge(m_split, j + 1)
            loop(dve, span, body, link, 4)

            def residual(name, square):
                span = SPANS[name]
                per = span.blocks // span.dtiles

                def body(i):
                    for c in range(span.blocks):
                        ahead(span, i, c)
                        if c % per == per - 1:
                            t = c // per
                            j = i * span.dtiles + t
                            x = one(X, j)
                            dve.wait_ge(block_done, blk(span, i, c) + (1 + RING))
                            tt(x, x, accD[(span.d0 + t) % 2][:], ALU.add).then_inc(evacD, 1)
                            dve.wait_ge(evacD, i * span.dtiles + (span.d0 + t + 3))
                            link(tt(square[:], x, x, ALU.mult))
                            link(tt(sums[:], sums[:], square[:], ALU.add))
                link(dve.memset(sums[:], 0.0))
                loop(dve, span, body, link, 2 * span.dtiles)
                dve.sem_inc(s_sq, 1)

            residual("w_o", norm_t)

            def normed_late(n, weight, done, outs=None):
                dve.wait_ge(s_root, n + 1)
                link(dve.reciprocal(root_late[:], root_late[:]))
                for k in range(KT):
                    if n == 2:
                        stt(X[:, k], X[:, k], col(weight, k), root_late[:], ALU.mult, ALU.mult).then_inc(x_scaled, 1)
                    elif outs is None:
                        link(stt(X[:, k], X[:, k], col(weight, k), root_late[:], ALU.mult, ALU.mult))
                        if n == 4 and k % 2:
                            dve.sem_inc(s_fin, 1)
                    else:
                        link(stt(norm_e[:], X[:, k], col(weight, k), root_late[:], ALU.mult, ALU.mult))
                        split(norm_e[:], outs[0][:, k], outs[1][:, k], s_split)
                        dve.wait_ge(s_split, done + k + 1)

            normed_late(1, "norm_ffn_w", KT, (u_high, u_low))

            span = SPANS["w_up"]
            dve.sem_inc(f_used, 2)

            def body(i):
                for c in range(span.blocks):
                    ahead(span, i, c)
                    j = i * 2 + c // 2
                    dve.wait_ge(evacA, i * 4 + (span.a0 + c + 3))
                    if c % 2 == 0:
                        taps = [col("ffn_conv_w", i * 2 + (k * FT + c // 2)) for k in range(3)]
                        link(causal(h1_conv[:], h1_raw[:], taps, col("ffn_conv_b", j)))
                        dve.sem_inc(f_conv, 1)
                        dve.sem_inc(f_used, 1)
                    else:
                        dve.wait_ge(f_silu, j + 1)
                        tt(h1_conv[:], h1_conv[:], h3_raw[:], ALU.mult).then_inc(f_used, 1)
                        dve.wait_ge(f_used, i * 4 + (2 * (c // 2) + 4))
                        split(h1_conv[:], one(f_high, j), one(f_low, j), f_split)
                        dve.wait_ge(f_split, j + 1)
            loop(dve, span, body, link, 8)
            residual("w_down", norm_f)
            normed_late(2, "final_norm_w", 0)
            normed_late(3, "norm_w_2", 2 * KT, (u_high, u_low))

            lbr = par[:, PCOL["lower_bounds_2"]:PCOL["lower_bounds_2"] + 2 * KT]
            tt(lbc[:, 1], lbr, lbr, ALU.subtract).then_inc(lb_v, 1)
            dve.wait_ge(lb_a, 1)
            link(dve.reciprocal(lbc[:, 2], lbc[:, 1]))
            link(tt(lbc[:, 1], lbc[:, 1], lbc[:, 2], ALU.mult))
            link(tt(lbc[:, 0], lbc[:, 1], lbc[:, 1], ALU.subtract))
            link(ts(lbc[:, 1], lbc[:, 0], -1.0, 1.0, ALU.mult, ALU.add))
            ts(lbc[:, 2], lbc[:, 0], LB_FLOOR, 2.0 ** 40, ALU.max, ALU.mult).then_inc(lb_v, 1)
            dve.wait_ge(lb_a, 3)
            link(ts(lbc[:, 2], lbc[:, 2], -40.0 * float(np.log(2.0)), None, ALU.add))
            link(tt(lbc[:, 3], lbc[:, 2], lbc[:, 1], ALU.subtract))
            link(tt(lbc[:, 4], lbc[:, 1], lbc[:, 2], ALU.subtract))

            span = SPANS["sg_v"]
            link(dve.memset(sums[:], 0.0))

            def body(i):
                for c in range(span.blocks):
                    ahead(span, i, c)
                    dve.wait_ge(evacA, i * 4 + (span.a0 + c + 3))
                    link(tt(sums[:], sums[:], one(VG, i * 4 + c), ALU.add))
            loop(dve, span, body, link, 4)
            dve.sem_inc(v_sum, 1)
            dve.wait_ge(v_mu, 1)
            link(dve.memset(sums[:], 0.0))
            span = SPANS["sg_u"]

            def body(i):
                for c in range(span.blocks):
                    ahead(span, i, c)
                    v = one(VG, i * 4 + c)
                    link(tt(v, v, ln_a[:], ALU.subtract))
                    link(tt(ln_b[:], v, v, ALU.mult))
                    link(tt(sums[:], sums[:], ln_b[:], ALU.add))
            loop(dve, span, body, link, 12)
            dve.sem_inc(v_sq, 1)
            dve.wait_ge(v_root, 1)
            link(dve.reciprocal(ln_a[:], ln_a[:]))
            span = SPANS["sg_gb"]
            dve.sem_inc(gs_used, 2)

            def body(i):
                for c in range(span.blocks):
                    ahead(span, i, c)
                    v, u = one(VG, i * 4 + c), one(UG, i * 4 + c)
                    link(stt(v, v, col("ln_w_2", i * 4 + c), ln_a[:], ALU.mult, ALU.mult))
                    dve.wait_ge(evacA, i * 4 + (span.a0 + c + 3))
                    tt(u, u, vn[:, c % 2], ALU.mult).then_inc(gs_used, 1)
                    dve.wait_ge(gs_used, i * 4 + (c + 3))
            loop(dve, span, body, link, 4)

            span = SPANS["mb"]
            dve.sem_inc(b_split, 1)

            def body(i):
                def finish(c):
                    j = i * 4 + c
                    dve.wait_ge(s_mix, j + 1)
                    link(tt(ln_b[:], one(UG, j), side[2][:], ALU.mult))
                    split(ln_b[:], one(b_high, j), one(b_low, j), b_split)
                    dve.wait_ge(b_split, j + 2)

                for c in range(span.blocks):
                    ahead(span, i, c)
                    j = i * 4 + c
                    ts(vn[:, c % 2], one(VG, j), col("ln_b_2", j), None, ALU.add).then_inc(vn_done, 1)
                    if c:
                        finish(c - 1)
                    dve.wait_ge(vn_turned, j + 1)
                    cp(vt[:, c % 2].rearrange("p c t -> p (c t)"), side[1][:]).then_inc(vt_done, 1)
                finish(3)
            loop(dve, span, body, link, 8)

            def scale(name, dst):
                span = SPANS[name]

                def body(i):
                    for c in range(span.blocks):
                        ahead(span, i, c)
                        m = one(dst, i * 4 + c)
                        dve.wait_ge(block_done, blk(span, i, c) + (1 + RING))
                        tt(m, m, accD[(span.d0 + c) % 2][:], ALU.mult).then_inc(evacD, 1)
                loop(dve, span, body)

            dve.wait_ge(evacA, 2 + SPANS["gla_first"].a0)
            scale("proj_b", M2)

            span = SPANS["gla"]
            link(dve.memset(att[:], 0.0))
            link(dve.memset(resets[:], 1.0))
            link(dve.memset(resets[:, 0::P], 0.0))
            dve.sem_inc(r_used, 1)
            dve.sem_inc(x_put, 2)
            dve.sem_inc(e_mul, 1)
            for c in range(4):
                ahead(SPANS["gla_first"], 0, c)

            def dve_gate(g2, g4, col_at, odd, step):
                G, Kd = Gs[odd], Kds[odd]
                for d in range(2):
                    if step == 0:
                        dve.wait_ge(l_ln, g2 + (d + 1))
                        link(stt(G[:, d], R[:, d], 0.0, G[:, d], ALU.min, ALU.subtract))
                        tt(Kd[:, d], G[:, d], R[:, d], ALU.subtract).then_inc(l_k, 1)
                    else:
                        dve.wait_ge(l_floor, g4 + (d + 3))
                        e = extra[d][:]
                        link(stt(e, G[:, d], col_at(3, d), e, ALU.max, ALU.add))
                        link(ts(e, e, col_at(1, d), None, ALU.add))
                        link(dve.tensor_tensor_scan(G[:, d], resets[:], e, 0.0, ALU.mult, ALU.add))
                        link(cp(tots[:, odd, d], G[:, d, P - 1::P]))
                        if d == 1:
                            link(tt(G[:, 1], G[:, 1], e, ALU.subtract))

            for step in range(2):
                dve_gate(0, 0, lambda k, d: lbc[:, k, d * KT:d * KT + 1], 0, step)

            def gcol(k, d, i, hh):
                n = i * 2 + (d * KT + hh)
                return lbc[:, k, n:n + 1] if isinstance(n, int) else lbc[:, k, bass.ds(n, 1)]

            def body(i):
                for hh in range(2):
                    h12, h2, h1 = i * 24 + 12 * hh, i * 4 + 2 * hh, i * 2 + hh

                    def aheads_at(place):
                        for c in LO_AT.get(place, ()):
                            if c < OWN or not last_head(i, hh):
                                ahead(span, i, 6 * hh + c)

                    def gate_at(place):
                        for step in GATE_DVE.get(place, ()):
                            if not last_head(i, hh):
                                dve_gate(h2 + 2, i * 8 + (4 * hh + 4), lambda k, d: gcol(k, d, i, hh + 1), 1 - hh, step)

                    G, Kd, tot = Gs[hh], Kds[hh], tots[:, hh]
                    aheads_at("start")
                    dve.wait_ge(evacA, i * 12 + (span.a0 + 6 * hh - 1 + 3))
                    link(ts(R[:, 2], R[:, 2], float(P) ** -0.5, None, ALU.mult))
                    Q = R[:, 2]

                    def halves(t, h):
                        return t.rearrange("p (b u t) -> p b u t", u=2, t=h)

                    def diff(n):
                        d, lev = n // 6, n % 6
                        g, x = G[:, d], XL[:, n % 3]
                        if n >= 3:
                            dve.wait_ge(x_mm, h12 + (n - 2))
                        if lev < 5:
                            h = LEVELS[lev]
                            gh, xh = halves(g, h), halves(x, h)
                            ref = (gh[:, :, 0, h - 1:h] if d == 0 else gh[:, :, 1, 0:1]).to_broadcast([P, T // (2 * h), h])
                            tt(xh[:, :, 0], ref, gh[:, :, 0], ALU.subtract)
                            tt(xh[:, :, 1], gh[:, :, 1], ref, ALU.subtract).then_inc(x_diff, 1)
                        else:
                            gb = g.rearrange("p (b t) -> p b t", t=BOTTOM)
                            link(tt(rsum[:], gb[:, :, 1], gb[:, :, 2], ALU.add))
                            stt(x.rearrange("p (b t) -> p b t", t=BOTTOM),
                                rsum[:].rearrange("p (b o) -> p b o", o=1).to_broadcast([P, T // BOTTOM, BOTTOM]),
                                -0.5, gb, ALU.mult, ALU.add).then_inc(x_diff, 1)

                    def pair(n):
                        d, lev = n // 6, n % 6
                        x, key = XL[:, n % 3], Kd[:, d]
                        dve.wait_ge(x_exp, h12 + (n + 1))
                        if lev < 5:
                            h = LEVELS[lev]
                            xh = halves(x, h)
                            a, b = (key, Q) if d == 0 else (Q, key)
                            tt(xh[:, :, 0], xh[:, :, 0], halves(a, h)[:, :, 0], ALU.mult)
                            tt(xh[:, :, 1], xh[:, :, 1], halves(b, h)[:, :, 1], ALU.mult).then_inc(x_pair, 1)
                        else:
                            tt(x, x, Q if d == 0 else key, ALU.mult)
                            tt(XL[:, 3], XL[:, 3], key if d == 0 else Q, ALU.mult).then_inc(x_pair, 1)

                    def put(n):
                        d, lev = n // 6, n % 6
                        dve.wait_ge(x_mm, h12 + (n + 1))
                        dve.wait_ge(x_put, h12 + (n + 2))
                        dve.sem_inc(x_clear, 1)
                        at = lev * T // 2
                        size = T // 2 if lev < 5 else T
                        mask = masks[:, d, at:at + size]
                        if lev < 5:
                            h = LEVELS[lev]
                            a = halves(att[:, d], h)[:, :, 1 - d]
                            data = side[n % 2][:, 0:size].rearrange("p (b t) -> p b t", t=h)
                            mask = mask.rearrange("p (b t) -> p b t", t=h)
                        else:
                            a, data = att[:, d], side[n % 2][:]
                        dve.copy_predicated(a, mask, data).then_inc(x_put, 1)

                    diff(0)
                    for n in range(12):
                        if n + 1 < 12:
                            diff(n + 1)
                        pair(n)
                        if n:
                            put(n - 1)
                        aheads_at(n)
                        gate_at(n)
                        if n == 3:
                            dve.wait_ge(v_turned, h1 + 1)
                            cp(v_tok[:].rearrange("p c t -> p (c t)"), side[2][:]).then_inc(v_taken, 1)
                    for d in range(2):
                        if d == 1:
                            put(11)
                        gt = G[:, d].rearrange("p (c t) -> p c t", t=P)
                        tt(XL[:, 2 * d + 1].rearrange("p (c t) -> p c t", t=P),
                           tot[:, d].rearrange("p (c o) -> p c o", o=1).to_broadcast([P, NCH, P]), gt,
                           ALU.subtract).then_inc(e_diff, 1)
                    for d in range(2):
                        a, b = (Q, Kd[:, 0]) if d == 0 else (Kd[:, 1], Q)
                        dve.wait_ge(e_exp, i * 12 + (6 * hh + 3 * d + 3))
                        tt(XL[:, 2 * d], XL[:, 2 * d], a, ALU.mult).then_inc(e_mul, 1)
                        tt(XL[:, 2 * d + 1], XL[:, 2 * d + 1], b, ALU.mult).then_inc(e_mul, 1)
                    aheads_at("edges")
                    for d in range(2):
                        dve.wait_ge(k_turned, h2 + (d + 1))
                        cp(k_tok[:].rearrange("p c t -> p (c t)"), side[2][:, 0:(NCH - 1) * P]).then_inc(k_taken, 1)
                        dve.wait_ge(st_mm, h2 + (d + 1))
                        order = (0, 1, 2) if d == 0 else (2, 1, 0)
                        for k, n in enumerate(order):
                            st = side[2][:, n * P:(n + 1) * P]
                            if k == 0:
                                ins = cp(Sd[:, d, n], st)
                            else:
                                c = n if d == 0 else n + 1
                                ins = stt(Sd[:, d, n], Sd[:, d, order[k - 1]], dtot[:, d, c:c + 1], st, ALU.mult, ALU.add)
                            if k < 2:
                                link(ins)
                        ins.then_inc(st_done, 1)
                    gate_at("out")
                    dve.wait_ge(o_mm, h1 + 1)
                    link(cp(head_o[:], side[3][:]))
                    tt(head_s[:], head_o[:], head_o[:], ALU.mult).then_inc(o_sq, 1)
                    dve.wait_ge(o_rstd, i * 4 + (2 * hh + 3))
                    link(stt(head_o[:], head_o[:], col("gnorm_w_2", 0), head_s[:], ALU.mult, ALU.mult))
                    dve.wait_ge(evacA, i * 12 + (span.a0 + 6 * hh + 3))
                    link(tt(one(Ya, h1), head_o[:], R[:, 4], ALU.mult))
                    dve.sem_inc(r_used, 1)
            loop(dve, span, body, link, 42)

            for k in range(KT):
                split(Ya[:, k], ya_high[:, k], ya_low[:, k], ya_split)
            dve.wait_ge(ya_split, KT)
            span = SPANS["proj_a"]

            def body(i):
                for c in range(span.blocks):
                    ahead(span, i, c)
                    j = i * 4 + c
                    dve.wait_ge(block_done, blk(span, i, c) + (1 + RING))
                    tt(sums[:], one(SA, j), accD[(span.d0 + c) % 2][:], ALU.mult).then_inc(evacD, 1)
                    dve.wait_ge(evacD, i * 4 + (span.d0 + c + 3))
                    link(tt(sums[:], sums[:], one(M2, j), ALU.add))
                    split(sums[:], one(n_high, j), one(u_low, j), n_split)
                    dve.wait_ge(n_split, j + 1)
            loop(dve, span, body, link, 8)
            residual("w_out", norm_e)
            normed_late(4, "final_norm_w_2", 0)

        @block.gpsimd
        def _(pool):
            pool.wait_ge(v_sum, 1)
            pool.dma_start(ws_t[:], ws_in).then_inc(s_ws, 16)
            pool.dma_start(bs_row[:], bs_in).then_inc(s_ws, 16)
            for k in range(0, KT, 2):
                pool.wait_ge(s_fin, k // 2 + 1)
                pool.dma_start(out.rearrange("(k p) t -> p k t", p=P)[:, k:k + 2], X[:, k:k + 2]).then_inc(s_out, 16)
            pool.wait_ge(s_out, KT // 2 * 16)


def cols(v, n):
    return np.asarray(v).reshape(-1, P).T


def consts():
    i = np.arange(P)
    return np.stack([np.eye(P), np.ones((P, P)), i[:, None] <= i[None, :]], 1).astype(np.float32)


def level_masks():
    t = np.arange(T) % P
    s = np.arange(P)[:, None]
    out = []
    for back in range(2):
        row = []
        for h in LEVELS:
            half = (t // h) % 2 == (0 if back else 1)
            q = t[half][None, :]
            row.append(s // (2 * h) == q // (2 * h))
            row[-1] = row[-1] & ((s // h) % 2 == (1 if back else 0))
        q = t[None, :]
        row.append((s // BOTTOM == q // BOTTOM) & ((s >= q) if back else (s <= q)))
        out.append(np.concatenate(row, 1))
    return np.stack(out, 1).astype(np.float32)


def weight_stream(w):
    def blocks(m, columns, rows=None):
        rows = np.arange(KT * P) if rows is None else rows
        return [m[rows][:, columns].reshape(KT, P, P).transpose(1, 0, 2)]

    def cut(m, start, j, k0=0):
        return [m[k0 * P:(k0 + KT) * P, start + j * P:start + (j + 1) * P].reshape(KT, P, P).transpose(1, 0, 2)]

    w_in, out = w["w_in"][0], []
    for j in range(KT):
        for at in (C_A, V_A, B_A):
            out += cut(w_in, at, j)
    out += blocks(w_in, list(range(DT, DT + HEADS)) + list(range(DT - P + HEADS, DT)))
    for j in range(KT):
        out += cut(w_in, GATE_A, j)
    for j in range(KT):
        out += cut(w["w_a_out"][0], 0, j)
    for g in range(GROUPS):
        out += cut(w_in, XBC + D_INNER, g) + cut(w_in, XBC + D_INNER + GROUPS * D_STATE, g)
        for at in (XBC, Z):
            for j in range(4):
                out += cut(w_in, at, 4 * g + j)
    for j in range(KT):
        out += cut(w_in, GATE_S, j)
    for j in range(KT):
        out += cut(w["w_s_out"][0], 0, j) + cut(w["w_s_out"][0], 0, j, KT)
    for j in range(KT):
        out += cut(w["w_o"][0], 0, j)
    for j in range(FT):
        out += cut(w["w_up"][0], 0, j) + cut(w["w_up"][0], D_FF, j)
    for j in range(KT):
        out += cut(w["w_down"][0], 0, j) + cut(w["w_down"][0], 0, j, KT) + cut(w["w_down"][0], 0, j, FT - KT)
    w2 = w["w_in_2"][0]
    for at in (V2, U2, GB2, MB2):
        for j in range(KT):
            out += cut(w2, at, j)
    for j in range(KT):
        out += cut(w["w_proj_b_2"][0], 0, j)
    for j in range(-1, KT):
        for at in (GA2, MA2):
            out += cut(w2, at, j) if j >= 0 else []
        for at in (FF2, FB2, I2, Q2):
            out += cut(w2, at, j + 1) if j < KT - 1 else []
    for name in ("w_proj_a_2", "w_out_2"):
        for j in range(KT):
            out += cut(w[name][0], 0, j)
    return out


def kernel(**inputs):
    import concourse.bacc as bacc
    from concourse.bass_utils import run_bass_kernel_spmd

    w = {k: np.asarray(v) for k, v in inputs.items()}
    stream = np.stack([b.reshape(P, KT * P) for b in weight_stream(w)[:NBLK]])
    pad = {k: np.zeros((P, 1), np.float32) for k in ("dt_bias", "a_log")}
    columns = []
    for name, n in PARAMS:
        v = w[name]
        if name in pad:
            pad[name][:HEADS, 0] = v[0]
            v = pad[name]
        elif name == "d_skip":
            v = cols(np.repeat(v[0], HEAD_DIM), n)
        else:
            v = cols(v, n)
        assert v.shape == (P, n), (name, v.shape)
        columns.append(v)
    arrays = {
        "x_t": np.ascontiguousarray(w["x"][0].T),
        "stream": stream,
        "params": np.ascontiguousarray(np.concatenate(columns, 1)),
        "consts": consts(),
        "masks": level_masks(),
        "spatial_w": np.ascontiguousarray(w["w_s_2"][0].transpose(2, 0, 1)),
        "spatial_b": np.ascontiguousarray(w["b_s_2"][0][None]),
    }
    nc = bacc.Bacc("TRN2", target_bir_lowering=False, num_devices=1)
    args = [nc.dram_tensor(k, a.shape, mybir.dt.from_np(a.dtype), kind="ExternalInput").ap() for k, a in arrays.items()]
    out = nc.dram_tensor("out_t", (D, T), F32, kind="ExternalOutput").ap()
    build(nc, *args, out)
    r = run_bass_kernel_spmd(nc, [arrays], core_ids=[0])
    return np.ascontiguousarray(np.asarray(r.results[0]["out_t"]).T)[None]
```
